# Optimizing a Trainium2 kernel written in Bass

```python
import math
import jax, jax.numpy as jnp
from jax import lax
import numpy as np

D_MODEL = 1024
BATCH = 1
SEQ = 512
DEPTH = 2

GRID_W = 64
CTX_LEN = 256
Q_BLOCK = 128
EPS = 1e-6
ROPE_BASE = 10000.0

H_A = 8
Q_LORA = 384
KV_LORA = 256
NOPE_A = 64
ROPE_A = 32
V_A = 64

H_B = 4
DH_B = 64
V_B = 2 * DH_B

D_FF = 2816
CONV_W = 3

QKV_B = H_B * 2 * DH_B
IN_W = Q_LORA + KV_LORA + ROPE_A + 3 * QKV_B + 2 * D_MODEL


def rms_norm(x, g):
    xf = x.astype(jnp.float32)
    y = xf * lax.rsqrt(jnp.mean(xf * xf, axis=-1, keepdims=True) + EPS)
    return (y * g.astype(jnp.float32)).astype(x.dtype)

def modulate(h, shift, scale):
    return h * (1.0 + scale) + shift

def axial_rope_tables(rows, cols, dr, dtype):
    q = dr // 4
    freqs = ROPE_BASE ** (-jnp.arange(q, dtype=jnp.float32) / q)
    ang = jnp.concatenate([rows[:, None] * freqs, cols[:, None] * freqs], axis=-1)
    return jnp.cos(ang)[:, None, :].astype(dtype), jnp.sin(ang)[:, None, :].astype(dtype)

def apply_axial_rope(x, cos, sin):
    q = x.shape[-1] // 4
    xr1, xr2, xc1, xc2 = jnp.split(x, 4, axis=-1)
    cr, cc = cos[..., :q], cos[..., q:]
    sr, sc = sin[..., :q], sin[..., q:]
    return jnp.concatenate([xr1 * cr - xr2 * sr, xr1 * sr + xr2 * cr,
                            xc1 * cc - xc2 * sc, xc1 * sc + xc2 * cc], axis=-1)

def map_query_blocks(fn, qs):
    B, S = qs[0].shape[:2]
    nb = S // Q_BLOCK
    blk = tuple(q.reshape(B, nb, Q_BLOCK, *q.shape[2:]).swapaxes(0, 1) for q in qs)
    out = lax.map(lambda qb: fn(*qb), blk)
    return out.swapaxes(0, 1).reshape(B, S, *out.shape[3:])

def mla_attend(qn, qr, kn, kr, v):
    scale = (NOPE_A + ROPE_A) ** -0.5

    def one(qnb, qrb):
        s = (jnp.einsum('bqhd,bkhd->bhqk', qnb, kn) + jnp.einsum('bqhr,bkr->bhqk', qrb, kr)).astype(jnp.float32)
        p = jax.nn.softmax(s * scale, axis=-1).astype(v.dtype)
        return jnp.einsum('bhqk,bkhe->bqhe', p, v)

    return map_query_blocks(one, (qn, qr))

def diff_attend(q1, q2, k1, k2, v, lam):
    scale = DH_B ** -0.5

    def one(q1b, q2b):
        s1 = jnp.einsum('bqhd,bkhd->bhqk', q1b, k1).astype(jnp.float32) * scale
        s2 = jnp.einsum('bqhd,bkhd->bhqk', q2b, k2).astype(jnp.float32) * scale
        p = jax.nn.softmax(s1, axis=-1) - lam * jax.nn.softmax(s2, axis=-1)
        return jnp.einsum('bhqk,bkhe->bqhe', p.astype(v.dtype), v)

    return map_query_blocks(one, (q1, q2))

def mixer_inputs(h, p, rope_a, rope_b):
    B, S, _ = h.shape
    z = h @ p['w_in']
    cuts = np.cumsum([Q_LORA, KV_LORA, ROPE_A, QKV_B, QKV_B, QKV_B, D_MODEL]).tolist()
    c_q, c_kv, k_r, dq, dk, dv, ga, gb = jnp.split(z, cuts, axis=-1)
    q = (rms_norm(c_q, p['g_q']) @ p['w_uq']).reshape(B, S, H_A, NOPE_A + ROPE_A)
    qn, qr = q[..., :NOPE_A], q[..., NOPE_A:]
    kv = (rms_norm(c_kv, p['g_kv']) @ p['w_ukv']).reshape(B, S, H_A, NOPE_A + V_A)
    kn, va = kv[..., :NOPE_A], kv[..., NOPE_A:]
    kr = k_r[:, :, None, :]
    dq = dq.reshape(B, S, H_B, 2, DH_B)
    dk = dk.reshape(B, S, H_B, 2, DH_B)
    q1, q2 = dq[..., 0, :], dq[..., 1, :]
    k1, k2 = dk[..., 0, :], dk[..., 1, :]
    vb = dv.reshape(B, S, H_B, V_B)
    if rope_a is not None:
        qr = apply_axial_rope(qr, *rope_a)
        kr = apply_axial_rope(kr, *rope_a)
        q1, q2, k1, k2 = (apply_axial_rope(t, *rope_b) for t in (q1, q2, k1, k2))
    return {'qn': qn, 'qr': qr, 'kn': kn, 'kr': kr[:, :, 0, :], 'va': va,
            'q1': q1, 'q2': q2, 'k1': k1, 'k2': k2, 'vb': vb, 'ga': ga, 'gb': gb}

def mixer_outputs(o_a, o_b, ga, gb, p, lam_init):
    B, S = o_a.shape[:2]
    y_a = o_a.reshape(B, S, H_A * V_A) @ p['w_br_a']
    o_b = rms_norm(o_b, p['g_sub']) * (1.0 - lam_init)
    y_b = o_b.reshape(B, S, H_B * V_B) @ p['w_br_b']
    merged = jax.nn.sigmoid(ga) * y_a + jax.nn.sigmoid(gb) * y_b
    return merged @ p['w_out']

def conv_ffn(h, p):
    u = h @ p['w_up']
    C = u.shape[-1]
    u = lax.conv_general_dilated(u, p['conv_w'][:, None, :], window_strides=(1,),
                                 padding=((CONV_W // 2, CONV_W // 2),),
                                 dimension_numbers=('NWC', 'WIO', 'NWC'),
                                 feature_group_count=C) + p['conv_b']
    a, b = jnp.split(u, 2, axis=-1)
    return (jax.nn.silu(a) * b) @ p['w_down']

def first_inputs(seed: int = 0) -> dict:
    key = jax.random.key(seed)
    ks = jax.random.split(key, 32)
    L, D, F = DEPTH, D_MODEL, D_FF

    def nrm(k, shape, scale):
        return jax.random.normal(k, shape, jnp.float32) * scale

    def gain(k, shape):
        return 1.0 + 0.02 * jax.random.normal(k, shape, jnp.float32)

    return {
        'x': nrm(ks[0], (BATCH, SEQ, D), 1.0),
        'c': nrm(ks[1], (BATCH, D), 1.0),
        'ctx': nrm(ks[2], (BATCH, CTX_LEN, D), 1.0),
        'c_ctx': nrm(ks[3], (D,), 1.0),
        'w_ada': nrm(ks[4], (L, D, 6 * D), 0.5 * D ** -0.5),
        'b_ada': nrm(ks[5], (L, 6 * D), 0.01),
        'g_mix': gain(ks[6], (L, D)),
        'g_ffn': gain(ks[7], (L, D)),
        'w_in': nrm(ks[8], (L, D, IN_W), D ** -0.5),
        'g_q': gain(ks[9], (L, Q_LORA)),
        'w_uq': nrm(ks[10], (L, Q_LORA, H_A * (NOPE_A + ROPE_A)), Q_LORA ** -0.5),
        'g_kv': gain(ks[11], (L, KV_LORA)),
        'w_ukv': nrm(ks[12], (L, KV_LORA, H_A * (NOPE_A + V_A)), KV_LORA ** -0.5),
        'lam_q1': nrm(ks[13], (L, DH_B), 0.1),
        'lam_k1': nrm(ks[14], (L, DH_B), 0.1),
        'lam_q2': nrm(ks[15], (L, DH_B), 0.1),
        'lam_k2': nrm(ks[16], (L, DH_B), 0.1),
        'g_sub': gain(ks[17], (L, V_B)),
        'w_br_a': nrm(ks[18], (L, H_A * V_A, D), (H_A * V_A) ** -0.5),
        'w_br_b': nrm(ks[19], (L, H_B * V_B, D), (H_B * V_B) ** -0.5),
        'w_out': nrm(ks[20], (L, D, D), D ** -0.5),
        'w_up': nrm(ks[21], (L, D, 2 * F), D ** -0.5),
        'conv_w': nrm(ks[22], (L, CONV_W, 2 * F), CONV_W ** -0.5),
        'conv_b': nrm(ks[23], (L, 2 * F), 0.01),
        'w_down': nrm(ks[24], (L, F, D), F ** -0.5),
        'g_final': gain(ks[25], (D,)),
    }

def first_block(x, c, ctx, c_ctx, w_ada, b_ada, g_mix, g_ffn, w_in, g_q, w_uq, g_kv, w_ukv,
              lam_q1, lam_k1, lam_q2, lam_k2, g_sub, w_br_a, w_br_b, w_out,
              w_up, conv_w, conv_b, w_down, g_final):
    B, S, D = x.shape
    ROWS = S // GRID_W
    rows = jnp.repeat(jnp.arange(ROWS), GRID_W).astype(jnp.float32)
    cols = jnp.tile(jnp.arange(GRID_W), ROWS).astype(jnp.float32)
    rope_a = axial_rope_tables(rows, cols, ROPE_A, x.dtype)
    rope_b = axial_rope_tables(rows, cols, DH_B, x.dtype)

    x_lat, x_ctx = x, ctx
    for l in range(DEPTH):
        last = l == DEPTH - 1
        p = {'w_in': w_in[l], 'g_q': g_q[l], 'w_uq': w_uq[l], 'g_kv': g_kv[l], 'w_ukv': w_ukv[l],
             'g_sub': g_sub[l], 'w_br_a': w_br_a[l], 'w_br_b': w_br_b[l], 'w_out': w_out[l],
             'w_up': w_up[l], 'conv_w': conv_w[l], 'conv_b': conv_b[l], 'w_down': w_down[l]}
        lam_init = 0.8 - 0.6 * math.exp(-0.3 * l)
        lam = (jnp.exp(jnp.sum(lam_q1[l].astype(jnp.float32) * lam_k1[l].astype(jnp.float32)))
               - jnp.exp(jnp.sum(lam_q2[l].astype(jnp.float32) * lam_k2[l].astype(jnp.float32)))
               + lam_init)

        mod_lat = (jax.nn.silu(c) @ w_ada[l] + b_ada[l])[:, None, :]
        mod_ctx = jax.nn.silu(c_ctx) @ w_ada[l] + b_ada[l]
        sh1, sc1, gt1, sh2, sc2, gt2 = jnp.split(mod_lat, 6, axis=-1)
        csh1, csc1, cgt1, csh2, csc2, cgt2 = jnp.split(mod_ctx, 6, axis=-1)

        h_lat = modulate(rms_norm(x_lat, g_mix[l]), sh1, sc1)
        h_ctx = modulate(rms_norm(x_ctx, g_mix[l]), csh1, csc1)
        pl = mixer_inputs(h_lat, p, rope_a, rope_b)
        pc = mixer_inputs(h_ctx, p, None, None)
        cat = lambda name: jnp.concatenate([pc[name], pl[name]], axis=1)
        o_a = mla_attend(pl['qn'], pl['qr'], cat('kn'), cat('kr'), cat('va'))
        o_b = diff_attend(pl['q1'], pl['q2'], cat('k1'), cat('k2'), cat('vb'), lam)
        o_lat = mixer_outputs(o_a, o_b, pl['ga'], pl['gb'], p, lam_init)
        if not last:
            oc_a = mla_attend(pc['qn'], pc['qr'], pc['kn'], pc['kr'], pc['va'])
            oc_b = diff_attend(pc['q1'], pc['q2'], pc['k1'], pc['k2'], pc['vb'], lam)
            o_ctx = mixer_outputs(oc_a, oc_b, pc['ga'], pc['gb'], p, lam_init)
            x_ctx = x_ctx + cgt1 * o_ctx
        x_lat = x_lat + gt1 * o_lat

        h_lat = modulate(rms_norm(x_lat, g_ffn[l]), sh2, sc2)
        x_lat = x_lat + gt2 * conv_ffn(h_lat, p)
        if not last:
            h_ctx = modulate(rms_norm(x_ctx, g_ffn[l]), csh2, csc2)
            x_ctx = x_ctx + cgt2 * conv_ffn(h_ctx, p)

    return rms_norm(x_lat, g_final)


N_EVEN = (DEPTH + 1) // 2
N_ODD = DEPTH // 2

POOL_WINDOWS = (2, 4, 8, 16)
POOL_GROUPS = 4
POOL_WIDTH = D_MODEL // 2
POOL_GDIM = POOL_WIDTH // POOL_GROUPS
SGU_GROUPS = 4
SGU_WIDTH = D_MODEL // 2
SGU_GDIM = SGU_WIDTH // SGU_GROUPS
SGU_CHUNK = 128
EVEN_IN = POOL_WIDTH + 2 * SGU_WIDTH
EVEN_MIX = POOL_WIDTH + SGU_WIDTH
NSA_HEADS = 8
NSA_KV_GROUPS = 2
NSA_HPG = NSA_HEADS // NSA_KV_GROUPS
NSA_HEAD_DIM = 64
NSA_WIDTH = NSA_HEADS * NSA_HEAD_DIM
NSA_KV_WIDTH = NSA_KV_GROUPS * NSA_HEAD_DIM
CMP_BLOCK = 32
CMP_STRIDE = 16
CMP_HIDDEN = 128
SEL_BLOCK = 64
SEL_TOPK = 16
WINDOW = 512
FORCE_SCORE = 1.0e4
ROPE_THETA = 500000.0
ROPE_DIM = NSA_HEAD_DIM // 4
RET_HEADS = 4
RET_HEAD_DIM = 128
RET_WIDTH = RET_HEADS * RET_HEAD_DIM
RET_CHUNK = 128
RET_THETA = 10000.0
ODD_IN = NSA_WIDTH + 6 * NSA_KV_WIDTH + 3 * NSA_HEADS + 4 * RET_WIDTH
ODD_MIX = NSA_WIDTH + RET_WIDTH
FFN_HIDDEN = -(-8 * D_MODEL // (3 * 256)) * 256
NEG_INF = -1.0e30


def rms_norm_2(x, g, eps=1e-6):
    xf = x.astype(jnp.float32)
    y = xf * lax.rsqrt(jnp.mean(xf * xf, axis=-1, keepdims=True) + eps)
    return (y * g.astype(jnp.float32)).astype(x.dtype)

def layer_norm(x, g, b, eps=1e-5):
    xf = x.astype(jnp.float32)
    mu = jnp.mean(xf, axis=-1, keepdims=True)
    var = jnp.mean(jnp.square(xf - mu), axis=-1, keepdims=True)
    return ((xf - mu) * lax.rsqrt(var + eps) * g.astype(jnp.float32) + b.astype(jnp.float32)).astype(x.dtype)

def masked_softmax(s, mask):
    return jax.nn.softmax(jnp.where(mask, s.astype(jnp.float32), NEG_INF), axis=-1)

def rope_tables(positions, rot_dim, theta):
    inv_freq = 1.0 / (theta ** (jnp.arange(0, rot_dim, 2, dtype=jnp.float32) / rot_dim))
    ang = positions.astype(jnp.float32)[..., None] * inv_freq
    return jnp.cos(ang)[:, None], jnp.sin(ang)[:, None]

def apply_rope(x, cos, sin):
    half = cos.shape[-1]
    x1, x2, rest = x[..., :half], x[..., half:2 * half], x[..., 2 * half:]
    c, s = cos.astype(x.dtype), sin.astype(x.dtype)
    return jnp.concatenate([x1 * c - x2 * s, x2 * c + x1 * s, rest], axis=-1)

def to_heads(x, n):
    b, t, _ = x.shape
    return x.reshape(b, t, n, -1).transpose(0, 2, 1, 3)

def swiglu(h, w_gate, w_up, w_down):
    return (jax.nn.silu(h @ w_gate) * (h @ w_up)) @ w_down

def pool_mixer(a, pool_w, pool_scale):
    b, t_len, _ = a.shape
    af = a.astype(jnp.float32).reshape(b, t_len, POOL_GROUPS, POOL_GDIM)
    cs = jnp.concatenate([jnp.zeros_like(af[:, :1]), jnp.cumsum(af, axis=1)], axis=1)
    t = jnp.arange(t_len)
    pooled = []
    for gi, w in enumerate(POOL_WINDOWS):
        lo = jnp.maximum(t + 1 - w, 0)
        win_sum = cs[:, 1:, gi] - cs[:, lo, gi]
        pooled.append(win_sum / (t + 1 - lo).astype(jnp.float32)[None, :, None])
    pooled = jnp.stack(pooled, axis=2)
    diff = (pooled - af).astype(a.dtype)
    y = jnp.einsum('btgc,gcd->btgd', diff, pool_w)
    return y.reshape(b, t_len, POOL_WIDTH) * pool_scale

def sgu_mixer(u, v, ln_g, ln_b, w_s, b_s):
    b, t_len, _ = u.shape
    u = jax.nn.gelu(u)
    v = layer_norm(jax.nn.gelu(v), ln_g, ln_b)
    n_chunk = t_len // SGU_CHUNK
    vc = v.reshape(b, n_chunk, SGU_CHUNK, SGU_GROUPS, SGU_GDIM)
    causal = jnp.tril(jnp.ones((SGU_CHUNK, SGU_CHUNK), dtype=bool))
    w_masked = jnp.where(causal[None], w_s, 0.0).astype(v.dtype)
    mixed = jnp.einsum('gts,bcsgd->bctgd', w_masked, vc) + b_s.T[None, None, :, :, None]
    return u * mixed.reshape(b, t_len, SGU_WIDTH)

def even_mixer(h, w_in, pool_w, pool_scale, sgu_ln_g, sgu_ln_b, sgu_w, sgu_b, w_out):
    z = h @ w_in
    a = z[..., :POOL_WIDTH]
    u = z[..., POOL_WIDTH:POOL_WIDTH + SGU_WIDTH]
    v = z[..., POOL_WIDTH + SGU_WIDTH:]
    y_a = pool_mixer(a, pool_w, pool_scale)
    y_b = sgu_mixer(u, v, sgu_ln_g, sgu_ln_b, sgu_w, sgu_b)
    return jnp.concatenate([y_a, y_b], axis=-1) @ w_out

def compress_blocks(k, pos_emb, w1, w2):
    t_len = k.shape[2]
    n_cmp = (t_len - CMP_BLOCK) // CMP_STRIDE + 1
    idx = np.arange(n_cmp)[:, None] * CMP_STRIDE + np.arange(CMP_BLOCK)[None, :]
    blocks = k[:, :, idx] + pos_emb
    flat = blocks.reshape(blocks.shape[:3] + (CMP_BLOCK * NSA_HEAD_DIM,))
    return jax.nn.gelu(flat @ w1) @ w2

def nsa_attention(q, k_cmp, v_cmp, k_sel, v_sel, k_win, v_win, gates, positions,
                  cmp_k_pos, cmp_k_w1, cmp_k_w2, cmp_v_pos, cmp_v_w1, cmp_v_w2):
    b, t_len, _ = q.shape
    G, M, d = NSA_KV_GROUPS, NSA_HPG, NSA_HEAD_DIM
    cos, sin = rope_tables(positions, ROPE_DIM, ROPE_THETA)
    q = apply_rope(to_heads(q, NSA_HEADS), cos, sin) * (d ** -0.5)
    k_cmp = apply_rope(to_heads(k_cmp, G), cos, sin)
    k_sel = apply_rope(to_heads(k_sel, G), cos, sin)
    k_win = apply_rope(to_heads(k_win, G), cos, sin)
    v_cmp, v_sel, v_win = to_heads(v_cmp, G), to_heads(v_sel, G), to_heads(v_win, G)

    kc = compress_blocks(k_cmp, cmp_k_pos, cmp_k_w1, cmp_k_w2)
    vc = compress_blocks(v_cmp, cmp_v_pos, cmp_v_w1, cmp_v_w2)
    n_cmp = kc.shape[2]
    cmp_end = jnp.arange(n_cmp) * CMP_STRIDE + CMP_BLOCK - 1

    n_sel = t_len // SEL_BLOCK
    top_k = min(SEL_TOPK, n_sel)
    c_start = np.arange(n_cmp) * CMP_STRIDE
    s_start = np.arange(n_sel) * SEL_BLOCK
    cmp_to_sel = ((c_start[:, None] < s_start[None, :] + SEL_BLOCK)
                  & (c_start[:, None] + CMP_BLOCK > s_start[None, :])).astype(np.float32)
    ks_blk = k_sel.reshape(b, G, n_sel, SEL_BLOCK, d)
    vs_blk = v_sel.reshape(b, G, n_sel, SEL_BLOCK, d)
    kw_pad = jnp.pad(k_win, ((0, 0), (0, 0), (WINDOW, 0), (0, 0)))
    vw_pad = jnp.pad(v_win, ((0, 0), (0, 0), (WINDOW, 0), (0, 0)))
    g = jax.nn.sigmoid(gates.astype(jnp.float32)).reshape(b, t_len, NSA_HEADS, 3)
    g = g.transpose(0, 2, 1, 3).astype(q.dtype)
    b_idx = jnp.arange(b)[:, None, None, None]
    g_idx = jnp.arange(G)[None, :, None, None]
    j_sel = jnp.arange(n_sel)

    def block(i):
        t0 = i * Q_BLOCK
        tq = t0 + jnp.arange(Q_BLOCK)
        qb = lax.dynamic_slice_in_dim(q, t0, Q_BLOCK, axis=2).reshape(b, G, M, Q_BLOCK, d)
        gb = lax.dynamic_slice_in_dim(g, t0, Q_BLOCK, axis=2)
        s = jnp.einsum('bgmqd,bgnd->bgmqn', qb, kc)
        p_cmp = masked_softmax(s, cmp_end[None, :] <= tq[:, None])
        p_cmp = p_cmp * (tq >= CMP_BLOCK - 1).astype(jnp.float32)[:, None]
        o_cmp = jnp.einsum('bgmqn,bgnd->bgmqd', p_cmp.astype(vc.dtype), vc)
        p_slc = jnp.einsum('bgmqn,nj->bgqj', p_cmp, cmp_to_sel)
        cur = tq // SEL_BLOCK
        sel_ok = j_sel[None, :] <= cur[:, None]
        forced = (j_sel[None, :] == 0) | (j_sel[None, :] == cur[:, None]) | (j_sel[None, :] == cur[:, None] - 1)
        score = jnp.where(sel_ok, jnp.where(forced, FORCE_SCORE, p_slc), -1.0)
        top_val, top_idx = lax.top_k(score, top_k)
        ks = ks_blk[b_idx, g_idx, top_idx]
        vs = vs_blk[b_idx, g_idx, top_idx]
        tok = top_idx[..., None] * SEL_BLOCK + jnp.arange(SEL_BLOCK)
        tok_ok = (top_val >= 0.0)[..., None] & (tok <= tq[:, None, None])
        s = jnp.einsum('bgmqd,bgqkld->bgmqkl', qb, ks).reshape(b, G, M, Q_BLOCK, top_k * SEL_BLOCK)
        p = masked_softmax(s, tok_ok.reshape(b, G, 1, Q_BLOCK, top_k * SEL_BLOCK))
        p = p.reshape(b, G, M, Q_BLOCK, top_k, SEL_BLOCK).astype(vs.dtype)
        o_sel = jnp.einsum('bgmqkl,bgqkld->bgmqd', p, vs)
        kwb = lax.dynamic_slice_in_dim(kw_pad, t0, WINDOW + Q_BLOCK, axis=2)
        vwb = lax.dynamic_slice_in_dim(vw_pad, t0, WINDOW + Q_BLOCK, axis=2)
        pos = t0 - WINDOW + jnp.arange(WINDOW + Q_BLOCK)
        win_ok = (pos[None, :] >= 0) & (pos[None, :] <= tq[:, None]) & (pos[None, :] > tq[:, None] - WINDOW)
        s = jnp.einsum('bgmqd,bgsd->bgmqs', qb, kwb)
        o_win = jnp.einsum('bgmqs,bgsd->bgmqd', masked_softmax(s, win_ok).astype(vwb.dtype), vwb)
        o = jnp.stack([o_cmp, o_sel, o_win], axis=-1).reshape(b, NSA_HEADS, Q_BLOCK, d, 3)
        return jnp.einsum('bhqdc,bhqc->bqhd', o, gb)

    out = lax.map(block, jnp.arange(t_len // Q_BLOCK))
    return out.transpose(1, 0, 2, 3, 4).reshape(b, t_len, NSA_WIDTH)

def retention(q, k, v, gate, positions, gn_g):
    b, t_len, _ = q.shape
    H, d, C = RET_HEADS, RET_HEAD_DIM, RET_CHUNK
    n_chunk = t_len // C
    cos, sin = rope_tables(positions, d, RET_THETA)
    q = apply_rope(to_heads(q, H), cos, sin)
    k = apply_rope(to_heads(k, H), cos, sin) * (d ** -0.5)
    v = to_heads(v, H)
    log_gamma = jnp.log1p(-jnp.exp2(-5.0 - jnp.arange(H, dtype=jnp.float32)))
    idx = jnp.arange(C, dtype=jnp.float32)
    rel = idx[:, None] - idx[None, :]
    decay = jnp.where(rel >= 0, jnp.exp(jnp.maximum(rel, 0.0)[None] * log_gamma[:, None, None]), 0.0)
    qc = q.reshape(b, H, n_chunk, C, d)
    kc = k.reshape(b, H, n_chunk, C, d)
    vc = v.reshape(b, H, n_chunk, C, d)
    s = jnp.einsum('bhcid,bhcjd->bhcij', qc, kc) * decay[None, :, None].astype(q.dtype)
    o_intra = jnp.einsum('bhcij,bhcje->bhcie', s, vc)
    zeta = jnp.exp((C - 1 - idx)[None, :] * log_gamma[:, None])
    chunk_kv = jnp.einsum('bhcjd,bhcje->bhcde', kc * zeta[None, :, None, :, None].astype(k.dtype), vc)
    g_chunk = jnp.exp(C * log_gamma)[None, :, None, None]

    def step(state, kv):
        return state * g_chunk + kv, state

    _, prev = lax.scan(step, jnp.zeros((b, H, d, d), jnp.float32),
                       jnp.moveaxis(chunk_kv, 2, 0).astype(jnp.float32))
    prev = jnp.moveaxis(prev, 0, 2)
    xi = jnp.exp((idx + 1.0)[None, :] * log_gamma[:, None])
    o_cross = jnp.einsum('bhcid,bhcde->bhcie', qc.astype(jnp.float32) * xi[None, :, None, :, None], prev)
    o = (o_intra.astype(jnp.float32) + o_cross).reshape(b, H, t_len, d).transpose(0, 2, 1, 3)
    mu = jnp.mean(o, axis=-1, keepdims=True)
    var = jnp.mean(jnp.square(o - mu), axis=-1, keepdims=True)
    o = ((o - mu) * lax.rsqrt(var + 1e-5)).reshape(b, t_len, RET_WIDTH) * gn_g.astype(jnp.float32)
    return (jax.nn.silu(gate.astype(jnp.float32)) * o).astype(gate.dtype)

def odd_mixer(h, positions, w_in, cmp_k_pos, cmp_k_w1, cmp_k_w2, cmp_v_pos, cmp_v_w1, cmp_v_w2,
              ret_gn_g, w_out):
    z = h @ w_in
    sizes = [NSA_WIDTH] + [NSA_KV_WIDTH] * 6 + [3 * NSA_HEADS] + [RET_WIDTH] * 4
    splits = np.cumsum(sizes)[:-1].tolist()
    q, kc, vc, ks, vs, kw, vw, gt, rq, rk, rv, rg = jnp.split(z, splits, axis=-1)
    y_c = nsa_attention(q, kc, vc, ks, vs, kw, vw, gt, positions,
                        cmp_k_pos, cmp_k_w1, cmp_k_w2, cmp_v_pos, cmp_v_w1, cmp_v_w2)
    y_d = retention(rq, rk, rv, rg, positions, ret_gn_g)
    return jnp.concatenate([y_c, y_d], axis=-1) @ w_out

def second_inputs(seed: int = 0) -> dict:
    key = jax.random.key(seed)
    ks = jax.random.split(key, 32)

    def nrm(k, shape, scale):
        return jax.random.normal(k, shape, jnp.float32) * scale

    def gain(k, shape):
        return 1.0 + 0.05 * jax.random.normal(k, shape, jnp.float32)

    NE, NO, D, F = N_EVEN, N_ODD, D_MODEL, FFN_HIDDEN
    x = nrm(ks[0], (BATCH, SEQ, D), 1.0)
    start = jax.random.randint(ks[1], (BATCH, 1), 0, 2048, dtype=jnp.int32)
    positions = start + jnp.arange(SEQ, dtype=jnp.int32)[None, :]
    cmp_in = CMP_BLOCK * NSA_HEAD_DIM
    return {
        "x": x,
        "positions": positions,
        "ln_mix_pre": gain(ks[2], (DEPTH, D)),
        "ln_mix_post": gain(ks[3], (DEPTH, D)),
        "ln_ffn_pre": gain(ks[4], (DEPTH, D)),
        "ln_ffn_post": gain(ks[5], (DEPTH, D)),
        "ffn_w_gate": nrm(ks[6], (DEPTH, D, F), D ** -0.5),
        "ffn_w_up": nrm(ks[7], (DEPTH, D, F), D ** -0.5),
        "ffn_w_down": nrm(ks[8], (DEPTH, F, D), F ** -0.5),
        "ev_w_in": nrm(ks[9], (NE, D, EVEN_IN), D ** -0.5),
        "ev_pool_w": nrm(ks[10], (NE, POOL_GROUPS, POOL_GDIM, POOL_GDIM), POOL_GDIM ** -0.5),
        "ev_pool_scale": 1.0 + 0.1 * jax.random.normal(ks[11], (NE, POOL_WIDTH), jnp.float32),
        "ev_sgu_ln_g": gain(ks[12], (NE, SGU_WIDTH)),
        "ev_sgu_ln_b": nrm(ks[13], (NE, SGU_WIDTH), 0.02),
        "ev_sgu_w": nrm(ks[14], (NE, SGU_GROUPS, SGU_CHUNK, SGU_CHUNK), SGU_CHUNK ** -0.5),
        "ev_sgu_b": 1.0 + 0.1 * jax.random.normal(ks[15], (NE, SGU_GROUPS, SGU_CHUNK), jnp.float32),
        "ev_w_out": nrm(ks[16], (NE, EVEN_MIX, D), EVEN_MIX ** -0.5),
        "od_w_in": nrm(ks[17], (NO, D, ODD_IN), D ** -0.5),
        "od_cmp_k_pos": nrm(ks[18], (NO, CMP_BLOCK, NSA_HEAD_DIM), 0.1),
        "od_cmp_k_w1": nrm(ks[19], (NO, cmp_in, CMP_HIDDEN), cmp_in ** -0.5),
        "od_cmp_k_w2": nrm(ks[20], (NO, CMP_HIDDEN, NSA_HEAD_DIM), CMP_HIDDEN ** -0.5),
        "od_cmp_v_pos": nrm(ks[21], (NO, CMP_BLOCK, NSA_HEAD_DIM), 0.1),
        "od_cmp_v_w1": nrm(ks[22], (NO, cmp_in, CMP_HIDDEN), cmp_in ** -0.5),
        "od_cmp_v_w2": nrm(ks[23], (NO, CMP_HIDDEN, NSA_HEAD_DIM), CMP_HIDDEN ** -0.5),
        "od_ret_gn_g": gain(ks[24], (NO, RET_WIDTH)),
        "od_w_out": nrm(ks[25], (NO, ODD_MIX, D), ODD_MIX ** -0.5),
    }

def second_block(x, positions, ln_mix_pre, ln_mix_post, ln_ffn_pre, ln_ffn_post,
              ffn_w_gate, ffn_w_up, ffn_w_down,
              ev_w_in, ev_pool_w, ev_pool_scale, ev_sgu_ln_g, ev_sgu_ln_b, ev_sgu_w, ev_sgu_b, ev_w_out,
              od_w_in, od_cmp_k_pos, od_cmp_k_w1, od_cmp_k_w2, od_cmp_v_pos, od_cmp_v_w1, od_cmp_v_w2,
              od_ret_gn_g, od_w_out):
    for layer in range(DEPTH):
        h = rms_norm_2(x, ln_mix_pre[layer])
        if layer % 2 == 0:
            e = layer // 2
            m = even_mixer(h, ev_w_in[e], ev_pool_w[e], ev_pool_scale[e], ev_sgu_ln_g[e],
                           ev_sgu_ln_b[e], ev_sgu_w[e], ev_sgu_b[e], ev_w_out[e])
        else:
            o = layer // 2
            m = odd_mixer(h, positions, od_w_in[o], od_cmp_k_pos[o], od_cmp_k_w1[o], od_cmp_k_w2[o],
                          od_cmp_v_pos[o], od_cmp_v_w1[o], od_cmp_v_w2[o], od_ret_gn_g[o], od_w_out[o])
        x = x + rms_norm_2(m, ln_mix_post[layer])
        h = rms_norm_2(x, ln_ffn_pre[layer])
        x = x + rms_norm_2(swiglu(h, ffn_w_gate[layer], ffn_w_up[layer], ffn_w_down[layer]), ln_ffn_post[layer])
    return x


def setup_inputs(seed=0):
    out = dict(first_inputs(seed))
    for name, value in second_inputs(seed + 1).items():
        if name != "x":
            out[name + "_2"] = value
    return out


def reference(
    x, c, ctx, c_ctx, w_ada, b_ada, g_mix, g_ffn, w_in, g_q, w_uq, g_kv, w_ukv, lam_q1, lam_k1,
    lam_q2, lam_k2, g_sub, w_br_a, w_br_b, w_out, w_up, conv_w, conv_b, w_down, g_final,
    positions_2, ln_mix_pre_2, ln_mix_post_2, ln_ffn_pre_2, ln_ffn_post_2, ffn_w_gate_2,
    ffn_w_up_2, ffn_w_down_2, ev_w_in_2, ev_pool_w_2, ev_pool_scale_2, ev_sgu_ln_g_2,
    ev_sgu_ln_b_2, ev_sgu_w_2, ev_sgu_b_2, ev_w_out_2, od_w_in_2, od_cmp_k_pos_2, od_cmp_k_w1_2,
    od_cmp_k_w2_2, od_cmp_v_pos_2, od_cmp_v_w1_2, od_cmp_v_w2_2, od_ret_gn_g_2, od_w_out_2,
):
    x = first_block(
        x, c, ctx, c_ctx, w_ada, b_ada, g_mix, g_ffn, w_in, g_q, w_uq, g_kv, w_ukv, lam_q1,
        lam_k1, lam_q2, lam_k2, g_sub, w_br_a, w_br_b, w_out, w_up, conv_w, conv_b, w_down,
        g_final,
    )
    return second_block(
        x, positions_2, ln_mix_pre_2, ln_mix_post_2, ln_ffn_pre_2, ln_ffn_post_2, ffn_w_gate_2,
        ffn_w_up_2, ffn_w_down_2, ev_w_in_2, ev_pool_w_2, ev_pool_scale_2, ev_sgu_ln_g_2,
        ev_sgu_ln_b_2, ev_sgu_w_2, ev_sgu_b_2, ev_w_out_2, od_w_in_2, od_cmp_k_pos_2,
        od_cmp_k_w1_2, od_cmp_k_w2_2, od_cmp_v_pos_2, od_cmp_v_w1_2, od_cmp_v_w2_2,
        od_ret_gn_g_2, od_w_out_2,
    )


_drawn_inputs = setup_inputs


def setup_inputs(seed=0):
    import zlib

    import numpy as np

    out = dict(_drawn_inputs(seed))
    spreads = {}
    factors = {'g_mix': 8.0,
     'g_ffn': 3.745,
     'g_q': 8.0,
     'g_kv': 8.0,
     'lam_q1': 7.201,
     'lam_k1': 8.0,
     'lam_q2': 6.692,
     'lam_k2': 7.873,
     'g_sub': 8.0,
     'conv_b': 8.0,
     'ev_sgu_ln_b_2': 6.504,
     'od_cmp_k_pos_2': 8.0}
    for name, (base, spread) in spreads.items():
        noise = np.random.default_rng([zlib.crc32(name.encode()), seed]).standard_normal(out[name].shape)
        drawn = base * np.exp(spread * noise) if base else spread * noise
        out[name] = __import__('jax').numpy.asarray(drawn.astype(out[name].dtype))
    for name, factor in factors.items():
        out[name] = (out[name] * factor).astype(out[name].dtype)
    return out
```

```python
import math
from contextlib import ExitStack

import concourse.bass as bass
import numpy as np
from concourse import mybir

P = 128
D = 1024
DC = D // P
N_LAT, N_CTX = 512, 256
N_TOK = N_LAT + N_CTX
CTX, LAT = (0, N_CTX), (N_CTX, N_TOK)
DEPTH = 2
GRID_W = 64
EPS = 1e-6

H_A, NOPE_A, ROPE_A, V_A = 8, 64, 32, 64
Q_LORA, KV_LORA = 384, 256
H_B, DH_B = 4, 64
F = 2816
FC = F // P
QKV_B = H_B * 2 * DH_B
Z_CQ, Z_CKV, Z_KR = 0, Q_LORA, Q_LORA + KV_LORA
Z_DQ = Z_KR + ROPE_A
Z_DK, Z_DV = Z_DQ + QKV_B, Z_DQ + 2 * QKV_B
Z_GA = Z_DQ + 3 * QKV_B
Z_GB = Z_GA + D

POOL_WINDOWS = (2, 4, 8, 16)
GC = 4
T2 = 512
TT = T2 // P
NSA_H, NSA_G, NSA_D = 8, 2, 64
CMP_BLOCK, CMP_STRIDE = 32, 16
N_CMP = (T2 - CMP_BLOCK) // CMP_STRIDE + 1
SEL_BLOCK, SEL_TOPK, WINDOW = 64, 16, 512
NSA_ROPE, NSA_THETA = NSA_D // 4, 500000.0
RET_H, RET_D, RET_THETA = 4, 128, 10000.0
O_Q = 0
O_KC, O_VC, O_KS, O_VS, O_KW, O_VW = (512 + 128 * i for i in range(6))
O_GT = 512 + 768
O_RQ = O_GT + 3 * NSA_H
O_RK, O_RV, O_RG = O_RQ + 512, O_RQ + 1024, O_RQ + 1536
assert SEL_TOPK >= T2 // SEL_BLOCK and WINDOW >= T2
MASKED = -1.0e30
ADA_ON_PE = (0, 2, 4)

ALU = mybir.AluOpType
ACT = mybir.ActivationFunctionType
AX = mybir.AxisListType
F32 = mybir.dt.float32
I32 = mybir.dt.int32

F32R = mybir.dt.float32r

SLOT = 2048
N_SLOTS = 2
HALF_FC = FC // 2
HEAD_Q, HEAD_KV = (NOPE_A + ROPE_A) * Q_LORA // P, (NOPE_A + V_A) * KV_LORA // P
BANK = 512


def blocks_of(name):
    def step(start, end, width):
        return [[(a, min(a + width, end))] for a in range(start, end, width)]

    if name == "w_ada":
        return step(0, 6 * D, 256)
    if name == "w_in":
        blocks = [[(Z_CQ, Z_CQ + 256)], [(Z_CQ + 256, Z_CKV)], [(Z_CKV, Z_KR)], [(Z_KR - 64, Z_DQ)]]
        for h in range(H_B):
            blocks.append([(z + h * P, z + (h + 1) * P) for z in (Z_DQ, Z_DK)])
            blocks.append([(Z_DV + h * P, Z_DV + (h + 1) * P)])
        return blocks + [[(Z_GA + a, Z_GA + a + P), (Z_GB + a, Z_GB + a + P)] for a in range(0, D, P)]
    if name == "w_uq":
        return step(0, H_A * (NOPE_A + ROPE_A), NOPE_A + ROPE_A)
    if name == "w_ukv":
        return step(0, H_A * (NOPE_A + V_A), NOPE_A + V_A)
    if name == "w_br":
        return [[(a, a + P), (D + a, D + a + P)] for a in range(0, D, P)]
    if name in ("w_up", "ffn_up"):
        return [[(a, a + P), (F + a, F + a + P)] for a in range(0, F, P)]
    if name in ("w_down", "ffn_down"):
        return step(0, D, P)
    if name in ("w_out", "ev_w_out", "od_w_out"):
        return step(0, D, 256)
    if name == "ev_w_in":
        return step(0, 1536, 256)
    if name == "od_w_in":
        return (step(0, O_VS, 256) + [[(O_VS, O_KW)], [(O_KW, O_VW)], [(O_VW, O_GT)], [(O_GT, O_RQ)]]
                + step(O_RQ, O_RG + 512, 256))
    if name == "cmp_w1":
        return [[(0, P)]]
    raise KeyError(name)


ROWS = {"w_ada": D, "w_in": D, "w_uq": Q_LORA, "w_ukv": KV_LORA, "w_br": 512, "w_out": D, "w_up": D,
        "w_down": F // 2, "ffn_up": D, "ffn_down": F // 2, "ev_w_in": D, "ev_w_out": D, "od_w_in": D, "od_w_out": D,
        "cmp_w1": CMP_BLOCK * NSA_D}
LAYERS = {n: 1 if n[:3] in ("ev_", "od_") else DEPTH for n in ROWS}
LAYERS["w_down"] = LAYERS["ffn_down"] = 2 * DEPTH


def block_table(name):
    nk, at, out = ROWS[name] // P, 0, []
    for _ in range(LAYERS[name]):
        for ranges in blocks_of(name):
            w = sum(b - a for a, b in ranges)
            out.append((at, nk, w))
            at += P * nk * w
    return out, at


VEC1 = [("g_mix", DC), ("g_ffn", DC), ("g_q", Q_LORA // P), ("g_kv", KV_LORA // P), ("g_sub", 1),
        ("b_ada", 6 * DC), ("conv_w", 3 * 2 * FC), ("conv_b", 2 * FC)]
VEC2 = [("mix_pre", DC), ("mix_post", DC), ("ffn_pre", DC), ("ffn_post", DC)]
VEC2X = [("pool_scale", GC), ("gn_g", RET_H), ("g_final", DC), ("k_pos", 16), ("v_pos", 16)]


def columns(spec):
    at, out = 0, {}
    for name, n in spec:
        out[name] = (at, at + n)
        at += n
    return out, at


C1, NV1 = columns(VEC1)
C2, NV2 = columns(VEC2)
C2X, NV2X = columns(VEC2X)

CONST1 = [("cos_b", N_LAT), ("sin_b", N_LAT), ("cos_a", N_LAT), ("sin_a", N_LAT), ("rot_b", P), ("rot_a", P)]
CONST2 = [("causal", P), ("cmp_mask", TT * N_CMP), ("rot_n", P), ("rot_r", P), ("freq_n", 1), ("freq_r", 1),
          ("cmp_ok", 1), ("pool_count", 4 * 16)]
K1, NK1 = columns(CONST1)
K2, NK2 = columns(CONST2)


class op:

    @staticmethod
    def matmul(*a, **k):
        return lambda e: e.matmul(*a, **k)

    @staticmethod
    def transpose(*a, **k):
        return lambda e: e.transpose(*a, **k)

    @staticmethod
    def activation(*a, **k):
        return lambda e: e.activation(*a, **k)

    @staticmethod
    def tensor_tensor(*a, **k):
        return lambda e: e.tensor_tensor(*a, **k)

    @staticmethod
    def tensor_scalar(*a, **k):
        return lambda e: e.tensor_scalar(*a, **k)

    @staticmethod
    def scalar_tensor_tensor(*a, **k):
        return lambda e: e.scalar_tensor_tensor(*a, **k)

    @staticmethod
    def tensor_reduce(*a, **k):
        return lambda e: e.tensor_reduce(*a, **k)

    @staticmethod
    def tensor_copy(*a, **k):
        return lambda e: e.tensor_copy(*a, **k)

    @staticmethod
    def reciprocal(*a, **k):
        return lambda e: e.reciprocal(*a, **k)

    @staticmethod
    def memset(*a, **k):
        return lambda e: e.memset(*a, **k)

    @staticmethod
    def tensor_tensor_reduce(*a, **k):
        return lambda e: e.tensor_tensor_reduce(*a, **k)

    @staticmethod
    def bn_stats(*a, **k):
        return lambda e: e.bn_stats(*a, **k)

    @staticmethod
    def bn_aggr(*a, **k):
        return lambda e: e.bn_aggr(*a, **k)

    @staticmethod
    def affine_select(*a, **k):
        return lambda e: e.affine_select(*a, **k)


class Line:

    def __init__(self, sem, in_turn=False):
        self.sem, self.count, self.steps, self.seen = sem, 0, [], {}
        self.in_turn = in_turn

    def wait(self, *tickets):
        for t in tickets:
            if t is None or self.seen.get(id(t[0]), 0) >= t[1]:
                continue
            self.seen[id(t[0])] = t[1]
            self.steps.append(lambda e, t=t: e.wait_ge(t[0], t[1]))

    def do(self, step, *after):
        self.wait(*after)
        if self.in_turn:
            self.wait(self.last)
        self.count += 1
        self.steps.append(lambda e: step(e).then_inc(self.sem, 1))
        return self.sem, self.count

    def silent(self, step):
        self.steps.append(step)

    def dma(self, dst, src, loaded):
        self.steps.append(lambda e: e.dma_start(dst, src).then_inc(loaded, 16))

    @property
    def last(self):
        return (self.sem, self.count) if self.count else None

    def run(self, engine):
        for step in self.steps:
            step(engine)


class Layout:

    def __init__(self, arena, start, end):
        self.arena, self.at, self.end = arena, start, end

    def __call__(self, *shape):
        n = int(np.prod(shape))
        a = self.at
        self.at += n
        assert self.at <= self.end, (self.at, self.end)
        v = self.arena[:, a:a + n]
        if len(shape) == 2:
            return v.rearrange("p (a b) -> p a b", a=shape[0])
        if len(shape) == 3:
            return v.rearrange("p (a b c) -> p a b c", a=shape[0], b=shape[1])
        return v


def build(nc, dram, out, plan, stop=None):
    with ExitStack() as ctx:
        n_stat = 6
        arena_n = 36800
        hid_at = 17856
        ws = ctx.enter_context(nc.sbuf_tensor("split_weights", [P, N_SLOTS * 2 * SLOT], F32R))
        ws = ws[:, :].rearrange("p (i s n) -> p i s n", i=N_SLOTS, s=2)
        hs = ctx.enter_context(nc.sbuf_tensor("split_inputs", [P, 2 * DC * N_TOK], F32R))
        with nc.sbuf_tensor("before_hidden", [P, hid_at], F32), \
                nc.sbuf_tensor("split_hidden", [P, 2 * HALF_FC * N_TOK], F32R) as hid:
            pass
        arena = ctx.enter_context(nc.sbuf_tensor("arena", [P, arena_n], F32))
        psum = ctx.enter_context(nc.psum_tensor("psum", [P, 8 * BANK], F32))

        def sem(name):
            return ctx.enter_context(nc.semaphore(name))

        pe, act, dve = (Line(sem(n)) for n in ("pe_done", "act_done", "dve_done"))
        pool = Line(sem("pool_done"), in_turn=True)
        sp = Line(sem("sp_unused"))
        slot_sem = [sem(f"slot_loaded_{i}") for i in range(N_SLOTS)]
        out_sem = sem("out_stored")

        def small_load(dst, src, *after):
            small = small_load.sem[small_load.n % 12]
            k = small_load.n // 12 + 1
            small_load.n += 1
            sp.wait(*after, (small, 16 * (k - 1)) if k > 1 else None)
            sp.dma(dst, src, small)
            return small, 16 * k
        small_load.sem = [sem(f"small_{i}") for i in range(12)]
        small_load.n = 0

        bank_free = {b: [] for b in range(8)}

        def take(b):
            pe.wait(*bank_free[b])
            bank_free[b] = []
            return psum[:, b * BANK:(b + 1) * BANK]

        class Ring:
            def __init__(self, banks):
                self.banks, self.n = banks, 0

            def next(self):
                b = self.banks[self.n % len(self.banks)]
                self.n += 1
                return b, take(b)

        def mm(dst, pairs, *after, each=()):
            pe.wait(*after)
            n = len(pairs)
            for i, (l, r) in enumerate(pairs):
                if each:
                    pe.wait(each[i])
                if i < n - 1:
                    pe.silent(op.matmul(dst, l, r, start=(i == 0), stop=False))
            return pe.do(op.matmul(dst, l, r, start=(n == 1), stop=True))

        def gather():
            marks = [q.last for q in (pe, act, dve, pool)]
            for q in (pe, act, dve, pool):
                q.wait(*marks)
            return marks

        def split(hi, lo, x, t, *free, eng=dve):
            t_hi = act.do(op.activation(hi, x, ACT.Copy), t, *free)
            t_lo = eng.do(op.tensor_tensor(lo, x, hi.bitcast(F32), ALU.subtract), t, t_hi, *free)
            return t_hi, t_lo

        def mm3(dst, pairs, *after, each=()):
            return mm(dst, [x for l, r in pairs for x in ((l[0], r[0]), (l[0], r[1]), (l[1], r[0]))], *after,
                      each=[t for t in each for _ in range(3)])

        common = Layout(arena, 0, arena_n)
        raw = [common(SLOT) for _ in range(N_SLOTS)]
        raw_free = [(i, []) for i in range(N_SLOTS)]
        raw_n = [0] * N_SLOTS
        split_free = [(i, []) for i in range(N_SLOTS)]
        tables = {n: block_table(n)[0] for n in ROWS}
        per_layer = {n: len(blocks_of(n)) for n in ROWS}
        used = []
        loads, prepared = [], []

        class Block:

            def __init__(self, name, layer, block, is_split):
                at, nk, w = tables[name][layer * per_layer[name] + block]
                assert nk * w <= SLOT
                self.slot, freed = raw_free.pop(0)
                raw_n[self.slot] += 1
                self.nk, self.w, self.is_split = nk, w, is_split
                self.raw = raw[self.slot][:, 0:nk * w]
                sp.wait(*freed)
                sp.dma(self.raw, dram[name][at:at + P * nk * w].rearrange("(p n) -> p n", p=P),
                       slot_sem[self.slot])
                self.ready = [(slot_sem[self.slot], 16 * raw_n[self.slot])]

            def prepare(self):
                if not self.is_split:
                    self.v = self.raw.rearrange("p (k w) -> p k w", k=self.nk)
                    return
                self.place, freed = split_free.pop(0)
                hi, lo = (ws[:, self.place, s, 0:self.nk * self.w] for s in range(2))
                self.ready = split(hi, lo, self.raw, self.ready[0], *freed)
                raw_free.append((self.slot, self.ready))
                self.hi, self.lo = (x.rearrange("p (k w) -> p k w", k=self.nk) for x in (hi, lo))

            def part(self, k, a, b):
                if not self.is_split:
                    return self.v[:, k, a:b]
                return self.hi[:, k, a:b], self.lo[:, k, a:b]

            def free(self, ticket):
                if self.is_split:
                    split_free.append((self.place, [ticket]))
                else:
                    raw_free.append((self.slot, [ticket]))

        planned = [0]

        def run_ahead():
            while raw_free and plan is not None and planned[0] < len(plan):
                loads.append(Block(*plan[planned[0]]))
                planned[0] += 1
            while loads and len(prepared) < 2 and (split_free or not loads[0].is_split):
                b = loads.pop(0)
                b.prepare()
                prepared.append(b)
                while raw_free and plan is not None and planned[0] < len(plan):
                    loads.append(Block(*plan[planned[0]]))
                    planned[0] += 1

        def Weights(name, layer, block, is_split=True):
            used.append((name, layer, block, is_split))
            if plan is None:
                b = Block(*used[-1])
                b.prepare()
                return b
            assert plan[len(used) - 1] == used[-1]
            if not prepared:
                run_ahead()
            b = prepared.pop(0)
            run_ahead()
            return b

        ident = common(P)
        ones = common(P)
        stats = common(n_stat, 6)
        stat_n = [0]
        silu_c = common(DC, 2)
        t_c = small_load(silu_c, dram["c_pair"].rearrange("(c p) t -> p c t", p=P))
        t_ident = small_load(ident, dram["ident"])
        pool.do(op.memset(ones, 1.0))
        eps_col = common(1)
        t_eps = pool.do(op.memset(eps_col, EPS))
        for q in (pe, act, dve, pool):
            q.wait(t_ident, t_eps)

        wide = common(2, D)
        row_all = common(2 * T2)
        row = row_all.rearrange("p (a b) -> p a b", a=2)
        rstd = common(2, T2)
        vec2 = common(DEPTH, NV2)
        vecx = common(NV2X)
        vec = common(DEPTH, NV1)
        common_end = common.at

        row_n, row_free, row_owner = [0], [[], []], [None, None]

        def next_row():
            i = row_n[0] % 2
            row_n[0] += 1
            if row_owner[i]:
                row_owner[i].flush()
            return i, row[:, i, :]

        rstd_free = [[], []]

        def rsqrt(out, total, n, *after, eps=None):
            eps = eps_col if eps is None else eps
            t = act.do(op.activation(out, total, ACT.Ln, bias=eps, scale=1.0 / n), *after)
            return act.do(op.activation(out, out, ACT.Exp, scale=-0.5), t)

        class Squares:

            def __init__(self, n, width, which=0, on_pool=False):
                self.n, self.width, self.which, self.c, self.pending = n, width, which, 0, []
                self.bank, self.ps, self.t_log = 6 + which, None, None
                self.on_pool, self.products = on_pool, 0

            def add(self, view, *after):
                if self.on_pool and self.c < self.n - 1:
                    acc = rstd[:, self.which, 0:view.shape[1]]
                    self.c += 1
                    if self.c == 1:
                        self.t_acc = act.do(op.activation(acc, view, ACT.Square), *after, *rstd_free[self.which])
                    else:
                        i, s = next_row()
                        s = s[:, 0:view.shape[1]]
                        t = act.do(op.activation(s, view, ACT.Square), *after, *row_free[i])
                        self.t_acc = pool.do(op.tensor_tensor(acc, acc, s, ALU.add), t, self.t_acc)
                        row_free[i] = [self.t_acc]
                    if self.c == self.n - 1:
                        self.pending.append((None, acc, self.t_acc))
                    return
                i, s = next_row()
                s = s[:, 0:view.shape[1]]
                t = act.do(op.activation(s, view, ACT.Square), *after, *row_free[i])
                self.pending.append((i, s, t))
                row_owner[i] = self

            def flush(self):
                for i, s, t in self.pending:
                    if self.ps is None:
                        self.ps = take(self.bank)[:, 0:s.shape[1]]
                    pe.wait(t)
                    if i is None:
                        self.t = pe.do(op.matmul(self.ps, ones, s, start=True, stop=False))
                        self.products += 1
                        continue
                    self.t = pe.do(op.matmul(self.ps, ones, s, start=(self.products == 0), stop=(self.c == self.n - 1)))
                    self.products += 1
                    self.c += 1
                    row_free[i] = [self.t]
                    row_owner[i] = None
                self.pending = []

            def log(self):
                self.flush()
                assert self.c == self.n
                r = rstd[:, self.which, 0:self.ps.shape[1]]
                self.t_log = act.do(op.activation(r, self.ps, ACT.Ln, bias=eps_col, scale=1.0 / self.width), self.t,
                                    *rstd_free[self.which])
                bank_free[self.bank].append(self.t_log)

            def finish(self):
                if self.t_log is None:
                    self.log()
                r = rstd[:, self.which, 0:self.ps.shape[1]]
                return r, act.do(op.activation(r, r, ACT.Exp, scale=-0.5), self.t_log)

        def apply_norm(sq, n, a, b, emit):
            r, t = sq.finish()
            done = {(c, a): emit(c, a, b, r, t) for c in range(n)}
            rstd_free[sq.which] = [dve.last, pool.last]
            return done

        lay = Layout(arena, common_end, arena_n)
        X = lay(DC, N_TOK)
        HS = hs[:, :].rearrange("p (s c t) -> p s c t", s=2, c=DC)
        HIDS = hid[:, :].rearrange("p (s c t) -> p s c t", s=2, c=HALF_FC)

        def h_part(k, a, b):
            return HS[:, 0, k, a:b], HS[:, 1, k, a:b]

        h_ready = {}

        def h_each(a):
            start = max(x for _, x in h_ready if x <= a)
            return [h_ready[c, start] for c in range(DC)]

        def hid_part(k, a, b):
            return HIDS[:, 0, k, a:b], HIDS[:, 1, k, a:b]

        const = lay(NK1)
        mods = [lay(6 * DC, 2) for _ in range(2)]
        gain = lay(2, DC, 2)
        lam_s = lay(DEPTH, 5)
        gsub_s = lay(DEPTH)
        region = lay.at

        def kc(name):
            a, b = K1[name]
            return const[:, a:b]

        def vc(name, j=0):
            return vec[:, layer, C1[name][0] + j:C1[name][0] + j + 1]

        all_banks = Ring(list(range(6)))
        t_silu = act.do(op.activation(silu_c, silu_c, ACT.Silu), t_c)

        scratch = Layout(arena, region, arena_n)
        first_w, t_first_w = [scratch(SLOT) for _ in range(8)], []
        for blk in range(8):
            at, nk, w = tables["w_ada"][blk]
            t_first_w.append(small_load(first_w[blk], dram["w_ada"][at:at + P * nk * w].rearrange("(p n) -> p n", p=P)))
            if blk == 0:
                t_wide = small_load(wide, dram["c_wide"])
            if blk == 5:
                x_src = dram["x_t"].rearrange("(c p) t -> p c t", p=P)
                t_x = {(c, a): small_load(X[:, c:c + 4, a:b], x_src[:, c:c + 4, a:b])
                       for a, b in (LAT, CTX) for c in (0, 4)}
        t_wide = act.do(op.activation(wide, wide, ACT.Silu), t_wide)

        def ada_pe(layer, blk):
            w = first_w[blk].rearrange("p (k n) -> p k n", k=DC)
            b, ps = all_banks.next()
            for j in range(2):
                t = mm(ps[:, 2 * j:2 * j + 2],
                       [(w[:, k, j * P:(j + 1) * P], silu_c[:, k, :]) for k in range(DC)], t_first_w[blk], t_silu)
            t = act.do(op.activation(
                mods[layer][:, 2 * blk:2 * blk + 2, :], ps[:, 0:4].rearrange("p (a b) -> p a b", b=2), ACT.Copy), t)
            bank_free[b].append(t)
            return t

        def ada_dot(layer, c, s, wt, *ready, junk=None):
            dot = [wt, wide[:, s, :], 1.0, 0.0, ALU.mult, ALU.add, mods[layer][:, c, s:s + 1]]
            if junk is not None:
                return dve.do(op.tensor_tensor_reduce(junk, *dot), *ready, t_wide, dve.last)
            t = dve.do(op.tensor_tensor_reduce(row_all, *dot), *ready, t_wide, *row_free[0], *row_free[1])
            row_free[0] = row_free[1] = [t]
            return t

        def ada_block(layer, blk, streams):
            w = Weights("w_ada", layer, blk, False)
            wt = w.raw.rearrange("p (j k) -> p j k", j=2)
            for j in range(2):
                t_dot = None
                if streams == 2 or j == 0:
                    t_dot = ada_dot(layer, 2 * blk + j, 0, wt[:, j, :], *w.ready)
                    yield
                if streams == 2 or j == 1:
                    s = streams - 1
                    t = pool.do(op.tensor_tensor(wt[:, j, :], wt[:, j, :], wide[:, s, :], ALU.mult), *w.ready,
                                t_wide, t_dot)
                    yield
                    t = act.do(op.activation(wt[:, j, :], wt[:, j, :], ACT.Copy,
                                             accum_out=mods[layer][:, 2 * blk + j, s:s + 1]), t)
            w.free(t)
            ada_ticket[layer] = [t, dve.last]

        def mods_done(layer, groups, streams, *after):
            m = mods[layer]
            for g in groups:
                for s in range(streams):
                    v = m[:, g * DC:(g + 1) * DC, s]
                    a = C1["b_ada"][0] + g * DC
                    t = dve.do(op.tensor_tensor(v, v, vec[:, layer, a:a + DC], ALU.add), *after)
            return t

        def mod(layer, g, c, s):
            return mods[layer][:, g * DC + c, s:s + 1]

        def make_gain(which, layer, g, gname, streams, t):
            a = C1[gname][0]
            for s in range(streams):
                t = dve.do(op.scalar_tensor_tensor(
                    out=gain[:, which, :, s], in0=mods[layer][:, g * DC:(g + 1) * DC, s], scalar=1.0,
                    in1=vec[:, layer, a:a + DC], op0=ALU.add, op1=ALU.mult), t)
            return t

        def modulate(layer, which, shift_group, t_mod):
            def emit(c, a, b, r, t):
                s = 0 if (a, b) == LAT else 1
                i, y = next_row()
                y = y[:, 0:b - a]
                t = dve.do(op.scalar_tensor_tensor(
                    out=y, in0=X[:, c, a:b], scalar=gain[:, which, c, s:s + 1], in1=r,
                    op0=ALU.mult, op1=ALU.mult), t, *row_free[i], t_mod)
                shift = mod(layer, shift_group, c, s)
                hi, lo = h_part(c, a, b)
                t_hi = act.do(op.activation(hi, y, ACT.Identity, bias=shift), t)
                t_lo = dve.do(op.scalar_tensor_tensor(out=lo, in0=y, scalar=shift, in1=hi.bitcast(F32),
                                                      op0=ALU.add, op1=ALU.subtract), t_hi)
                row_free[i] = [t_lo]
                return t_lo
            return emit

        t_vec = small_load(vec, dram["vec1"].rearrange("l p n -> p l n"))
        junk = scratch(D)
        lam_q, lam_k, lam_p = scratch(2, 2, 64), scratch(2, 2, 64), scratch(2, 2, 64)
        t_l1 = small_load(lam_q, dram["lam"][:, 0].rearrange("l p a n -> p l a n"))
        t_l2 = small_load(lam_k, dram["lam"][:, 1].rearrange("l p a n -> p l a n"))
        ada_ticket = {}
        for blk in range(8):
            if blk in ADA_ON_PE:
                t = ada_pe(0, blk)
                continue
            for j in range(2):
                for s in range(2):
                    t2 = ada_dot(0, 2 * blk + j, s, first_w[blk][:, j * D:(j + 1) * D], t_first_w[blk],
                                 junk=junk)
        first = [t, t2]
        squares = {}
        for k, (a, b) in enumerate((LAT, CTX)):
            squares[a] = Squares(DC, D, k)
            for c in range(DC):
                squares[a].add(X[:, c, a:b], t_x[c // 4 * 4, a])
                squares[a].flush()
        t_const = small_load(const, dram["const1"])
        t_v2 = small_load(vec2, dram["vec2"].rearrange("l p n -> p l n"))
        t_vx = small_load(vecx, dram["vec2x"])
        for q in (pe, act, dve, pool):
            q.wait(t_vec, t_const, t_v2, t_vx)
        t = dve.do(op.tensor_tensor(lam_p, lam_q, lam_k, ALU.mult), t_l1, t_l2)
        t = dve.do(op.tensor_reduce(lam_s[:, :, 0:2], lam_p, AX.X, ALU.add), t)
        t = act.do(op.activation(lam_s[:, :, 2:4], lam_s[:, :, 0:2], ACT.Exp), t)
        lam_inits = [0.8 - 0.6 * math.exp(-0.3 * l) for l in range(DEPTH)]
        for l, lam_init in enumerate(lam_inits):
            t_lam = dve.do(op.scalar_tensor_tensor(
                out=lam_s[:, l, 4:5], in0=lam_s[:, l, 3:4], scalar=-lam_init, in1=lam_s[:, l, 2:3], op0=ALU.add,
                op1=ALU.subtract), t)

        for layer in range(DEPTH):
            last = layer == DEPTH - 1
            both = [LAT, CTX]
            mine = [LAT] if last else both
            lam_init = lam_inits[layer]
            t_gs = dve.do(op.tensor_scalar(gsub_s[:, layer:layer + 1], vc("g_sub"), 1.0 - lam_init, None, ALU.mult))

            t = mods_done(layer, [0, 1], 2, *first)
            t_mod = make_gain(0, layer, 1, "g_mix", 2, t)
            if plan is not None and not prepared:
                run_ahead()
            squares[N_CTX].log(), squares[0].log()
            for a, b in both:
                h_ready |= apply_norm(squares[a], DC, a, b, modulate(layer, 0, 0, t_mod))

            lay = Layout(arena, region, arena_n)
            CQ, CKV = lay(Q_LORA // P, N_TOK), lay(KV_LORA // P, N_TOK)
            KR = lay(N_TOK)
            QH, KH = lay(2, N_TOK), lay(2, N_TOK)
            VH = [lay(6, P) for _ in range(2)]
            PR = lay(4, N_TOK)
            PT = lay(2, N_TOK)
            OA = lay(4, N_TOK)
            OB = arena[:, region:region + 4 * N_TOK].rearrange("p (c t) -> p c t", c=4)
            assert Q_LORA + KV_LORA >= 4 * P
            rope_tmp = lay(2, N_LAT)
            head_w = [lay(HEAD_Q + HEAD_KV) for _ in range(2)]

            def in_place(view, gname):
                def emit(c, a, b, r, t):
                    return dve.do(op.scalar_tensor_tensor(
                        out=view[:, c, a:b], in0=view[:, c, a:b], scalar=vc(gname, c), in1=r,
                        op0=ALU.mult, op1=ALU.mult), t)
                return emit

            compressed = []
            for parts, dst, ranges, gname in ((((0, 0, 2), (1, 2, 1)), CQ, mine, "g_q"), (((2, 0, 2),), CKV, both, "g_kv")):
                n = dst.shape[1]
                sqs = {a: Squares(n, n * P, k) for k, (a, b) in enumerate(ranges)}
                for blk, m0, mn in parts:
                    w = Weights("w_in", layer, blk)
                    for m in range(mn):
                        for a, b in ranges:
                            bank, ps = all_banks.next()
                            t = mm3(ps[:, 0:b - a], [(w.part(k, m * P, (m + 1) * P), h_part(k, a, b)) for k in range(DC)],
                                    *w.ready, each=h_each(a))
                            sqs[a].flush()
                            t = act.do(op.activation(dst[:, m0 + m, a:b], ps[:, 0:b - a], ACT.Copy), t)
                            bank_free[bank].append(t)
                            sqs[a].add(dst[:, m0 + m, a:b], t)
                    w.free(pe.last)
                for a, b in ranges:
                    sqs[a].log()
                for a, b in ranges:
                    compressed += apply_norm(sqs[a], n, a, b, in_place(dst, gname)).values()
            kr = slice(NOPE_A, NOPE_A + ROPE_A)
            w = Weights("w_in", layer, 3)
            for a, b in both:
                bank, ps = all_banks.next()
                t = mm3(ps[0:kr.stop, 0:b - a], [(w.part(k, 0, kr.stop), h_part(k, a, b)) for k in range(DC)], *w.ready,
                        each=h_each(a))
                t = act.do(op.activation(KR[kr, a:b], ps[kr, 0:b - a], ACT.Copy), t)
                bank_free[bank].append(t)
            w.free(pe.last)

            rope_n = [0]
            rope_free = [None, None]
            t_kr_ctx = act.last

            def rope(view, rows, rot, cos, sin, ring, t_in):
                i = rope_n[0] % 2
                rope_n[0] += 1
                bank, ps = ring.next()
                tmp = rope_tmp[rows, i, :]
                t = mm(ps[rows, :], [(rot[rows, 0:rows.stop - rows.start], view)], t_in)
                t2 = dve.do(op.tensor_tensor(tmp, ps[rows, :], sin[rows, :], ALU.mult), t, rope_free[i])
                bank_free[bank].append(t2)
                t = dve.do(op.tensor_tensor(view, view, cos[rows, :], ALU.mult), t)
                t = dve.do(op.tensor_tensor(view, view, tmp, ALU.add), t, t2)
                rope_free[i] = t
                return t

            t_kr = rope(KR[kr, N_CTX:N_TOK], kr, kc("rot_a"), kc("cos_a"), kc("sin_a"), all_banks, act.last)
            pe.wait(t_kr, *compressed)

            gen = Ring([4, 5, 7])
            O_BANK = 6
            head_ready, v_ready = {}, {}
            buf_free = [[], []]
            heads = [("A", h) for h in range(H_A)] + [("B", h) for h in range(H_B)]

            def ada_jobs():
                for blk in range(8, 24):
                    yield from ada_block(layer, blk, len(mine))
                if not last:
                    for blk in range(8):
                        yield from ada_block(layer + 1, blk, 2)

            ada_steps = ada_jobs()
            ob_norm, ob_ready, oa_ready = [], [], []

            def norm_ob():
                while ob_norm:
                    h, a, b, i, s, t = ob_norm.pop(0)
                    ob = OB[:, h, a:b]
                    bank, ps = gen.next()
                    t = mm(ps[:, 0:b - a], [(ones, s)], t)
                    t = rsqrt(s, ps[:, 0:b - a], P, t)
                    bank_free[bank].append(t)
                    t = dve.do(op.scalar_tensor_tensor(out=ob, in0=ob, scalar=gsub_s[:, layer:layer + 1], in1=s,
                                                       op0=ALU.mult, op1=ALU.mult), t, t_gs)
                    row_free[i] = [t]
                    ob_ready.append(t)

            head_w_loaded = {}

            def load_head_w(h, *after):
                head_w_loaded[h] = []
                for name, a, n_ in (("w_uq", 0, HEAD_Q), ("w_ukv", HEAD_Q, HEAD_KV)):
                    at, _, _ = tables[name][layer * H_A + h]
                    head_w_loaded[h].append(small_load(head_w[h % 2][:, a:a + n_], dram[name][at:at + P * n_].rearrange(
                        "(p n) -> p n", p=P), *after))

            for h in range(2):
                load_head_w(h, act.last, dve.last, pe.last)

            def pieces(n):
                kind, h = heads[n]
                i = n % 2
                q, k, v = QH[:, i, :], KH[:, i, :], VH[i]
                ready = []
                head_ready[n] = ready

                def project(dst, m, a, b, product, pairs, *w_ready):
                    bank, ps = gen.next()
                    t = product(ps[0:m, 0:b - a], pairs, *w_ready)
                    t = act.do(op.activation(dst[0:m, a:b], ps[0:m, 0:b - a], ACT.Copy), t, *buf_free[i])
                    bank_free[bank].append(t)
                    return t

                def proj_a():
                    d = NOPE_A + ROPE_A
                    both_w, loaded = head_w[i], head_w_loaded[h]
                    w_q = both_w[:, 0:HEAD_Q].rearrange("p (k n) -> p k n", k=Q_LORA // P)
                    w_kv = both_w[:, HEAD_Q:HEAD_Q + HEAD_KV].rearrange("p (k n) -> p k n", k=KV_LORA // P)
                    for a, b in mine:
                        t = project(q, d, a, b, mm, [(w_q[:, kk, :], CQ[:, kk, a:b]) for kk in range(3)], *loaded)
                        if (a, b) == LAT:
                            tr = t
                        ready.append(t)
                        yield
                    for a, b in both:
                        ready.append(project(k, NOPE_A, a, b, mm,
                                             [(w_kv[:, kk, 0:NOPE_A], CKV[:, kk, a:b]) for kk in range(2)]))
                    if h < 2:
                        ready.append(dve.do(op.tensor_copy(k[kr, :], KR[kr, :]), t_kr, t_kr_ctx, *buf_free[i]))
                    yield
                    ready.append(rope(q[kr, N_CTX:N_TOK], kr, kc("rot_a"), kc("cos_a"), kc("sin_a"), gen, tr))
                    bank, ps = gen.next()
                    for t6 in range(6):
                        t = mm(ps[:, t6 * V_A:(t6 + 1) * V_A],
                               [(CKV[:, kk, t6 * P:(t6 + 1) * P], w_kv[:, kk, NOPE_A:]) for kk in range(2)])
                    if h + 2 < H_A:
                        load_head_w(h + 2, t)
                    t = dve.do(op.tensor_copy(
                        v[:, :, 0:V_A], ps[:, 0:6 * V_A].rearrange("p (t e) -> p t e", t=6)), t, *buf_free[i])
                    bank_free[bank].append(t)
                    v_ready[n] = [t]
                    yield

                def proj_b():
                    w = Weights("w_in", layer, 4 + 2 * h)
                    for a, b in mine:
                        t = project(q, P, a, b, mm3, [(w.part(kk, 0, P), h_part(kk, a, b)) for kk in range(DC)], *w.ready)
                        ready.append(t)
                        if (a, b) == LAT:
                            tq = t
                        yield
                    for a, b in both:
                        t = project(k, P, a, b, mm3, [(w.part(kk, P, 2 * P), h_part(kk, a, b)) for kk in range(DC)])
                        ready.append(t)
                        if (a, b) == LAT:
                            tk = t
                        yield
                    w.free(pe.last)
                    ready.append(rope(q[:, N_CTX:N_TOK], slice(0, P), kc("rot_b"), kc("cos_b"), kc("sin_b"), gen, tq))
                    ready.append(rope(k[:, N_CTX:N_TOK], slice(0, P), kc("rot_b"), kc("cos_b"), kc("sin_b"), gen, tk))
                    yield
                    w = Weights("w_in", layer, 5 + 2 * h)
                    for t0, tn in ((0, 4), (4, 2)):
                        bank, ps = gen.next()
                        for j in range(tn):
                            a = (t0 + j) * P
                            t = mm3(ps[:, j * P:(j + 1) * P],
                                    [(h_part(kk, a, a + P), w.part(kk, 0, P)) for kk in range(DC)], *w.ready)
                        if t0:
                            w.free(t)
                        t = dve.do(op.tensor_copy(
                            v[:, t0:t0 + tn, :], ps[:, 0:tn * P].rearrange("p (t e) -> p t e", t=tn)), t, *buf_free[i])
                        bank_free[bank].append(t)
                        v_ready.setdefault(n, []).append(t)
                        yield

                return proj_a() if kind == "A" else proj_b()

            pr_free = [None] * 4
            pt_free = [None, None]
            stat_free = [None] * n_stat

            def next_stat():
                i = stat_n[0] % n_stat
                stat_n[0] += 1
                return i, stats[:, i, :]

            def softmax_rows(s_ps, n, scale, p_dst, p_free, t_scores, s_bank, accum, accum_free):
                si, st = next_stat()
                t = dve.do(op.tensor_reduce(st[:, 0:1], s_ps[:, 0:n], AX.X, ALU.max), t_scores, stat_free[si])
                t = dve.do(op.tensor_scalar(st[:, 1:2], st[:, 0:1], -scale, None, ALU.mult), t)
                t = act.do(op.activation(p_dst[:, 0:n], s_ps[:, 0:n], ACT.Exp, bias=st[:, 1:2], scale=scale,
                                         accum_out=accum), t, p_free, accum_free)
                for b in s_bank:
                    bank_free[b].append(t)
                stat_free[si] = t
                return t

            def scores(u):
                n, kind, h, (ra, rb), qt, nkeys = u["n"], u["kind"], u["h"], u["rng"], u["qt"], u["nk"]
                i = n % 2
                q0 = ra + qt * P
                pe.wait(*head_ready[n])
                k_sp = [(0, min(nkeys, 512))] + ([(512, nkeys)] if nkeys > 512 else [])
                if kind == "A":
                    d = NOPE_A + ROPE_A
                    bp = 2 * (u["i"] % 2)
                    take(bp), take(bp + 1)
                    s = psum[:, bp * BANK:(bp + 2) * BANK]
                    for a, b in k_sp:
                        t = mm(s[:, a:b], [(QH[0:d, i, q0:q0 + P], KH[0:d, i, a:b])])
                    j = 2 * (u["i"] % 2)
                    u["p"] = PR[:, j, :]
                    u["pj"] = [j]
                    si, st = next_stat()
                    t = softmax_rows(s, nkeys, d ** -0.5, u["p"], pr_free[j], t, (bp, bp + 1), st[:, 0:1], stat_free[si])
                    next(ada_steps, None)
                    t = dve.do(op.reciprocal(st[:, 1:2], st[:, 0:1]), t)
                    p = u["p"][:, 0:nkeys]
                    u["t"] = stat_free[si] = dve.do(op.tensor_scalar(p, p, st[:, 1:2], None, ALU.mult), t)
                    return
                si, st = next_stat()
                ts = []
                j0 = 2 * (u["i"] % 2)
                for sub in range(2):
                    bp = 2 * sub
                    take(bp), take(bp + 1)
                    s = psum[:, bp * BANK:(bp + 2) * BANK]
                    rows = slice(sub * DH_B, (sub + 1) * DH_B)
                    for a, b in k_sp:
                        t = mm(s[:, a:b], [(QH[rows, i, q0:q0 + P], KH[rows, i, a:b])])
                    ts.append(softmax_rows(s, nkeys, DH_B ** -0.5, PR[:, j0 + sub, :], pr_free[j0 + sub], t,
                                           (bp, bp + 1), st[:, sub:sub + 1], stat_free[si]))
                next(ada_steps, None)
                t = dve.do(op.reciprocal(st[:, 2:4], st[:, 0:2]), *ts)
                t1 = dve.do(op.tensor_scalar(st[:, 4:5], st[:, 3:4], lam_s[:, layer, 4:5], None, ALU.mult), t, t_lam)
                t0 = act.do(op.activation(PR[:, j0, 0:nkeys], PR[:, j0, 0:nkeys], ACT.Copy,
                                                   scale=st[:, 2:3]), t)
                t = dve.do(op.scalar_tensor_tensor(
                    out=PR[:, j0, 0:nkeys], in0=PR[:, j0 + 1, 0:nkeys], scalar=st[:, 4:5], in1=PR[:, j0, 0:nkeys],
                    op0=ALU.mult, op1=ALU.add), t0, t1)
                stat_free[si] = t
                u["p"], u["pj"], u["t"] = PR[:, j0, :], [j0, j0 + 1], t

            def turn(u):
                kt = u["nk"] // P
                j = u["i"] % 2
                pt = PT[:, j, :]
                copied = []
                for t0 in range(0, kt, 4):
                    tn = min(4, kt - t0)
                    bank, ps = gen.next()
                    pe.wait(u["t"])
                    for x in range(tn):
                        t = pe.do(op.transpose(
                            ps[:, x * P:(x + 1) * P], u["p"][:, (t0 + x) * P:(t0 + x + 1) * P], ident))
                    eng = dve if t0 == 0 else act
                    if t0 == 0:
                        t = dve.do(op.tensor_copy(
                            pt[:, t0 * P:(t0 + tn) * P], ps[:, 0:tn * P]), t, pt_free[j])
                    else:
                        t = act.do(op.activation(
                            pt[:, t0 * P:(t0 + tn) * P], ps[:, 0:tn * P], ACT.Copy), t, pt_free[j])
                    bank_free[bank].append(t)
                    copied.append(t)
                for x in u["pj"]:
                    pr_free[x] = pe.last
                u["pt"], u["copied"] = pt, copied
                norm_ob()

            def values(u):
                n, kind, h, (ra, rb), qt, nkeys = u["n"], u["kind"], u["h"], u["rng"], u["qt"], u["nk"]
                i, j, kt, pt = n % 2, u["i"] % 2, nkeys // P, u["pt"]
                if qt == 0:
                    take(O_BANK)
                o = psum[:, O_BANK * BANK:(O_BANK + 1) * BANK]
                if kind == "A":
                    r0 = (h % 2) * V_A
                    o = o[r0:r0 + V_A, :]

                def v_of(x):
                    return VH[i][:, x, 0:V_A] if kind == "A" else VH[i][:, x, :]
                t = mm(o[:, qt * P:(qt + 1) * P],
                       [(v_of(x), pt[:, x * P:(x + 1) * P]) for x in range(kt)], *u["copied"], *v_ready[n])
                pt_free[j] = t
                if u["last_of_range"]:
                    w_ = rb - ra
                    if kind == "A":
                        t1 = act.do(op.activation(OA[r0:r0 + V_A, h // 2, ra:rb], o[:, 0:w_], ACT.Copy), t)
                        oa_ready.append(t1)
                    else:
                        t1 = act.do(op.activation(OB[:, h, ra:rb], o[:, 0:w_], ACT.Copy), t)
                        s_i, sq = next_row()
                        sq = sq[:, 0:w_]
                        ob_norm.append((h, ra, rb, s_i, sq, act.do(op.activation(sq, OB[:, h, ra:rb], ACT.Square), t1,
                                                                   *row_free[s_i])))
                    bank_free[O_BANK].append(t1)
                if u["last_of_head"]:
                    buf_free[i] = [t]

            units = []
            for n, (kind, h) in enumerate(heads):
                mine_units = []
                for rng in mine:
                    nq = (rng[1] - rng[0]) // P
                    for qt in range(nq):
                        mine_units.append(dict(n=n, kind=kind, h=h, rng=rng, qt=qt, nk=N_TOK if rng == LAT else N_CTX,
                                               last_of_range=qt == nq - 1, last_of_head=False, index=len(mine_units)))
                mine_units[-1]["last_of_head"] = True
                units += mine_units
            per_head = len(units) // len(heads)
            for i, u in enumerate(units):
                u["i"] = i
            for _ in pieces(0):
                pass
            queue = None
            br_at = (region + 22 * N_TOK + 2 * N_LAT, region + 22 * N_TOK)
            w_br = [arena[:, a:a + 1024].rearrange("p (k n) -> p k n", k=4) for a in br_at]
            br_loaded = {}

            def load_br(m, *after):
                at, nk, w = tables["w_br"][layer * DC + m]
                br_loaded[m] = small_load(w_br[m % 2], dram["w_br"][at:at + P * nk * w].rearrange(
                    "(p k n) -> p k n", p=P, k=nk), *after)

            for i, u in enumerate(units):
                if i == len(units) - per_head:
                    for m in range(2):
                        load_br(m, pe.last, dve.last)
                scores(u)
                if i > 1:
                    values(units[i - 2])
                if u["index"] == 2 and u["n"] + 1 < len(heads):
                    queue = list_steps = pieces(u["n"] + 1)
                    total = 7 if heads[u["n"] + 1][0] == "A" else 9
                if queue is not None and u["index"] >= 2 and u["n"] + 1 < len(heads):
                    k = -(-total // (per_head - 2))
                    for _ in range(k):
                        next(queue, None)
                if i > 0:
                    turn(units[i - 1])
                if layer == 0:
                    next(ada_steps, None)
                if u["last_of_head"]:
                    if queue is not None:
                        for _ in queue:
                            pass
                        queue = None
            values(units[-2])
            turn(units[-1])
            values(units[-1])
            norm_ob()
            for _ in ada_steps:
                pass
            if not last:
                first = ada_ticket[layer + 1]
            t = mods_done(layer, [2, 3, 4, 5], len(mine), *ada_ticket[layer])
            t_mod = make_gain(1, layer, 4, "g_ffn", len(mine), t)
            for q in (dve, act):
                q.wait(t_mod)

            lay2 = Layout(arena, region + 5 * N_TOK, arena_n)
            MG = lay2(DC, N_TOK)
            PG = lay2(4, N_TOK)
            assert lay2.at <= region + 22 * N_TOK + 0
            prods = PG
            sg_free = [[None, None], [None, None]]
            merged = {}
            step = 0
            for m in range(DC):
                wg = Weights("w_in", layer, 4 + 2 * H_B + m)
                for a, b in mine:
                    n_ = b - a
                    i = step % 2
                    step += 1
                    sums = []
                    for g in range(2):
                        bank, ps = all_banks.next()
                        t = mm3(ps[:, 0:n_], [(wg.part(k, g * P, (g + 1) * P), h_part(k, a, b)) for k in range(DC)],
                                *wg.ready)
                        sg = prods[:, 2 * i + g, 0:n_]
                        t_sg = act.do(op.activation(sg, ps[:, 0:n_], ACT.Sigmoid), t, sg_free[i][g])
                        bank_free[bank].append(t_sg)
                        src = (OA, OB)[g]
                        pe.wait(*(oa_ready, ob_ready)[g])
                        bank, ps = all_banks.next()
                        t = mm(ps[:, 0:n_], [(w_br[m % 2][:, k, g * P:(g + 1) * P], src[:, k, a:b]) for k in range(4)],
                               br_loaded[m])
                        t = dve.do(op.tensor_tensor(sg, sg, ps[:, 0:n_], ALU.mult), t, t_sg)
                        bank_free[bank].append(t)
                        sums.append(t)
                    t = pool.do(op.tensor_tensor(
                        MG[:, m, a:b], prods[:, 2 * i, 0:n_], prods[:, 2 * i + 1, 0:n_], ALU.add), *sums)
                    sg_free[i] = [t, t]
                    merged[m, a] = t
                wg.free(pe.last)
                if m + 2 < DC:
                    load_br(m + 2, pe.last)
            squares = {a: Squares(DC, D, k, on_pool=True) for k, (a, b) in enumerate(mine)}
            t_used = pe.last
            for a, b in mine:
                for k in range(DC):
                    merged[k, a] = split(*h_part(k, a, b), MG[:, k, a:b], merged[k, a], t_used,
                                         eng=(dve, pool)[k % 2])[1]
            for pair in range(DC // 2):
                w = Weights("w_out", layer, pair)
                for j in range(2):
                    m = 2 * pair + j
                    for a, b in mine:
                        s = 0 if (a, b) == LAT else 1
                        bank, ps = all_banks.next()
                        t = mm3(ps[:, 0:b - a], [(w.part(k, j * P, (j + 1) * P), h_part(k, a, b)) for k in range(DC)],
                                *w.ready, each=[merged[k, a] for k in range(DC)])
                        squares[a].flush()
                        t = dve.do(op.scalar_tensor_tensor(
                            out=X[:, m, a:b], in0=ps[:, 0:b - a], scalar=mod(layer, 2, m, s), in1=X[:, m, a:b],
                            op0=ALU.mult, op1=ALU.add), t)
                        bank_free[bank].append(t)
                        squares[a].add(X[:, m, a:b], t)
                w.free(pe.last)
            assert region <= hid_at
            lay = Layout(arena, hid_at + 2 * HALF_FC * N_TOK, arena_n)
            ya, yb = lay(2, N_LAT), lay(2, N_LAT)
            for a, b in mine:
                squares[a].log()
            for a, b in mine:
                h_ready |= apply_norm(squares[a], DC, a, b, modulate(layer, 1, 3, t_mod))
            y_free = [[], []]
            step = 0
            hid_ready = {}
            for half in range(2):
                for m in range(HALF_FC):
                    w = Weights("w_up", layer, half * HALF_FC + m)
                    for a, b in mine:
                        n_ = b - a
                        i = step % 2
                        step += 1
                        conv = []
                        for g, y in ((0, ya), (1, yb)):
                            bank, ps = all_banks.next()
                            ch = g * FC + half * HALF_FC + m
                            t = mm3(ps[:, 0:n_], [(w.part(k, g * P, (g + 1) * P), h_part(k, a, b)) for k in range(DC)],
                                    *w.ready, each=h_each(a))
                            yv = y[:, i, 0:n_]
                            t = act.do(op.activation(
                                yv, ps[:, 0:n_], ACT.Identity, bias=vc("conv_b", ch), scale=vc("conv_w", 2 * FC + ch)),
                                t, *y_free[i])
                            t = dve.do(op.scalar_tensor_tensor(
                                out=yv[:, 1:n_], in0=ps[:, 0:n_ - 1], scalar=vc("conv_w", ch), in1=yv[:, 1:n_],
                                op0=ALU.mult, op1=ALU.add), t)
                            t = dve.do(op.scalar_tensor_tensor(
                                out=yv[:, 0:n_ - 1], in0=ps[:, 1:n_], scalar=vc("conv_w", 4 * FC + ch),
                                in1=yv[:, 0:n_ - 1], op0=ALU.mult, op1=ALU.add), t)
                            bank_free[bank].append(t)
                            conv.append(t)
                        ya_, yb_ = ya[:, i, 0:n_], yb[:, i, 0:n_]
                        t = act.do(op.activation(ya_, ya_, ACT.Silu), conv[0])
                        t = pool.do(op.tensor_tensor(ya_, ya_, yb_, ALU.mult), t, conv[1])
                        y_free[i] = split(*hid_part(m, a, b), ya_, t)
                        hid_ready[m, a] = y_free[i][1]
                    w.free(pe.last)
                if half == 1:
                    squares = {a: Squares(DC, D, k, on_pool=True) for k, (a, b) in enumerate(mine)}
                for m in range(DC):
                    w = Weights("w_down", 2 * layer + half, m)
                    for a, b in mine:
                        s = 0 if (a, b) == LAT else 1
                        bank, ps = all_banks.next()
                        t = mm3(ps[:, 0:b - a], [(w.part(k, 0, P), hid_part(k, a, b)) for k in range(HALF_FC)], *w.ready,
                                each=[hid_ready[k, a] for k in range(HALF_FC)])
                        if half == 1:
                            squares[a].flush()
                        t = dve.do(op.scalar_tensor_tensor(
                            out=X[:, m, a:b], in0=ps[:, 0:b - a], scalar=mod(layer, 5, m, s), in1=X[:, m, a:b],
                            op0=ALU.mult, op1=ALU.add), t)
                        bank_free[bank].append(t)
                        if half == 1:
                            squares[a].add(X[:, m, a:b], t)
                    w.free(pe.last)
            if stop == ("b1", layer):
                break

        marks = [q.last for q in (pe, act, dve, pool)]
        lay = Layout(arena, common_end, arena_n)
        X1 = X
        X = Layout(arena, arena_n - DC * T2, arena_n)(DC, T2)
        mixer_end = arena_n - DC * T2
        lay.at = common_end + DC * N_TOK
        con2 = lay(NK2)
        assert lay.at <= hid_at
        work1 = Layout(arena, common_end, common_end + DC * N_TOK)
        work2 = Layout(arena, lay.at, mixer_end)
        MX = Layout(arena, common_end, common_end + DC * T2)(DC, T2)
        HIDS2 = hid[:, 0:2 * HALF_FC * T2].rearrange("p (s c t) -> p s c t", s=2, c=HALF_FC)

        def hid2_part(k, a, b):
            return HIDS2[:, 0, k, a:b], HIDS2[:, 1, k, a:b]

        t_con2 = small_load(con2, dram["const2"], *marks)

        def v2(name, j=0):
            return vec2[:, layer, C2[name][0] + j:C2[name][0] + j + 1]

        def vx(name, j=0, n=1):
            return vecx[:, C2X[name][0] + j:C2X[name][0] + j + n]

        def k2(name):
            a, b = K2[name]
            return con2[:, a:b]

        ALL = (0, T2)

        def emit_final(c, a, b, r, t):
            return dve.do(op.scalar_tensor_tensor(out=X[:, c, :], in0=X1[:, c, a:b], scalar=vx("g_final", c),
                                                           in1=r, op0=ALU.mult, op1=ALU.mult), t)
        def new_squares(src, each):
            sq = Squares(DC, D)
            for c in range(DC):
                sq.add(src[:, c, 0:T2], each[c])
                sq.flush()
            return sq

        if stop is None or stop[0] == "b2":
            x_ready = apply_norm(squares[N_CTX], DC, *LAT, emit_final)
            x_ready = [x_ready[c, N_CTX] for c in range(DC)]
            squares = new_squares(X, x_ready)
            for q in (pe, act, dve, pool):
                q.wait(t_con2)
        else:
            squares[N_CTX].flush()
            for c in range(DC):
                dve.do(op.tensor_copy(X[:, c, :], X1[:, c, N_CTX:N_TOK]), act.last, dve.last)

        def pre_norm(squares, gname):
            def emit(c, a, b, r, t):
                i, y = next_row()
                t = dve.do(op.scalar_tensor_tensor(
                    out=y, in0=X[:, c, :], scalar=v2(gname, c), in1=r, op0=ALU.mult, op1=ALU.mult), t, *row_free[i])
                row_free[i] = split(*h_part(c, 0, T2), y, t)
                return row_free[i][1]
            return apply_norm(squares, DC, *ALL, emit)

        def post_norm(squares, gname):
            def emit(c, a, b, r, t):
                t = dve.do(op.scalar_tensor_tensor(
                    out=MX[:, c, :], in0=MX[:, c, :], scalar=v2(gname, c), in1=r, op0=ALU.mult, op1=ALU.mult), t)
                return pool.do(op.tensor_tensor(X[:, c, :], X[:, c, :], MX[:, c, :], ALU.add), t)
            ready = apply_norm(squares, DC, *ALL, emit)
            return new_squares(X, [ready[c, 0] for c in range(DC)])

        def project(w, col, x, consume, nk=DC):
            bank, ps = all_banks.next()
            if w.is_split:
                each = h_each(0) if x is h_part else [hid_ready[k, 0] for k in range(nk)]
                t = mm3(ps, [(w.part(k, col, col + P), x(k, 0, T2)) for k in range(nk)], *w.ready, each=each)
            else:
                t = mm(ps, [(w.part(k, col, col + P), x[:, k, :]) for k in range(nk)], *w.ready,
                       each=[y_ready[k] for k in range(nk)])
            bank_free[bank].append(consume(ps, t))

        def copy_to(dst):
            return lambda ps, t: act.do(op.activation(dst, ps, ACT.Copy), t)

        def out_linear(name, x):
            t_used = pe.last
            for k in range(DC):
                h_ready[k, 0] = split(*h_part(k, 0, T2), x[:, k, :], y_ready[k], t_used, eng=(dve, pool)[k % 2])[1]
            sq = Squares(DC, D, on_pool=True)
            for pair in range(DC // 2):
                w = Weights(name, 0, pair)
                for j in range(2):
                    project(w, j * P, h_part, copy_to(MX[:, 2 * pair + j, :]))
                    sq.flush()
                    sq.add(MX[:, 2 * pair + j, :], act.last)
                w.free(pe.last)
            return sq

        def token_major(w, width, consume):
            for tt in range(TT):
                bank, ps = all_banks.next()
                t = mm3(ps[:, 0:width], [(h_part(k, tt * P, (tt + 1) * P), w.part(k, 0, width)) for k in range(DC)],
                        *w.ready, each=h_each(0))
                bank_free[bank].append(consume(tt, ps[:, 0:width], t))

        def even_mixer(marks):
            L1 = Layout(arena, work1.at, work1.end)
            L2 = Layout(arena, work2.at, mixer_end)
            Y = L2(DC, T2)
            A, U, V = L1(GC, T2), L1(GC, T2), L1(TT, T2)
            gb, bs, wst, pw = L2(2, T2), L2(GC, P), L2(GC, P), L2(GC, P)
            S = [L2(T2) for _ in range(4)]
            bn = L2(TT, 6)
            mv = L2(TT, 2)
            eps5 = L2(1)
            t_eps = pool.do(op.memset(eps5, 1e-5), *marks)
            t_gb = small_load(gb, dram["sgu_gb"], *marks)
            t_bs = small_load(bs, dram["sgu_bs"], *marks)
            t_ws = small_load(wst, dram["sgu_wt"].rearrange("g s t -> s g t"), *marks)
            t_pw = small_load(pw, dram["pool_w"].rearrange("g a b -> a g b"), *marks)
            t_ws = pool.do(op.affine_select(out=wst, in_=wst, compare_op=ALU.is_ge, fill=0.0, base=0,
                                                     pattern=[[0, GC], [1, P]], channel_multiplier=-1), t_ws)
            for pair in range(2):
                w = Weights("ev_w_in", 0, pair)
                for j in range(2):
                    project(w, j * P, h_part, copy_to(A[:, 2 * pair + j, :]))
                w.free(pe.last)
            for pair in range(2):
                w = Weights("ev_w_in", 0, 2 + pair)
                for j in range(2):
                    project(w, j * P, h_part, lambda ps, t, c=2 * pair + j: act.do(
                        op.activation(U[:, c, :], ps, ACT.Gelu_apprx_tanh), t))
                w.free(pe.last)
            for pair in range(2):
                w = Weights("ev_w_in", 0, 4 + pair)
                token_major(w, 256, lambda tt, ps, t, a=256 * pair: act.do(
                    op.activation(V[:, tt, a:a + 256], ps, ACT.Gelu_apprx_tanh), t))
                w.free(pe.last)
            for tt in range(TT):
                v = V[:, tt, :]
                t = dve.do(op.bn_stats(bn[:, tt, :], v), act.last)
                t = dve.do(op.bn_aggr(mv[:, tt, :], bn[:, tt, :]), t)
                t = act.do(op.activation(mv[:, tt, 1:2], mv[:, tt, 1:2], ACT.Sqrt, bias=eps5[:, 0:1]), t, t_eps)
                t = dve.do(op.reciprocal(mv[:, tt, 1:2], mv[:, tt, 1:2]), t)
                t = dve.do(op.tensor_scalar(v, v, mv[:, tt, 0:1], mv[:, tt, 1:2], ALU.subtract,
                                                                 ALU.mult), t)
                t = pool.do(op.tensor_tensor(v, v, gb[:, 0, :], ALU.mult), t, t_gb)
                t = pool.do(op.tensor_tensor(v, v, gb[:, 1, :], ALU.add), t)
            t_v = t
            for g, win in enumerate(POOL_WINDOWS):
                src, t = A[:, g, :], act.last
                k, i = 1, 0
                while k < win:
                    dst = S[i % 2 + 2 * (g % 2)]
                    t_a = dve.do(op.tensor_tensor(
                        dst[:, k:T2], src[:, k:T2], src[:, 0:T2 - k], ALU.add), t, *([pool_free[g % 2]] if i < 2 else []))
                    t = dve.do(op.tensor_copy(dst[:, 0:k], src[:, 0:k]), t_a)
                    src, k, i = dst, 2 * k, i + 1
                cnt = K2["pool_count"][0] + 16 * g
                dst = S[i % 2 + 2 * (g % 2)]
                t = dve.do(op.tensor_tensor(
                    src[:, 0:16], src[:, 0:16], con2[:, cnt:cnt + 16], ALU.mult), t)
                t = dve.do(op.scalar_tensor_tensor(
                    out=dst, in0=src, scalar=1.0 / win, in1=A[:, g, :], op0=ALU.mult, op1=ALU.subtract), t,
                    pool_free[g % 2])
                bank, ps = all_banks.next()
                t = mm(ps, [(pw[:, g, :], dst)], t, t_pw)
                pool_free[g % 2] = t
                t = act.do(op.activation(Y[:, g, :], ps, ACT.Copy, scale=vx("pool_scale", g)), t)
                bank_free[bank].append(t)
                y_ready[g] = t
            for g in range(GC):
                bank, ps = all_banks.next()
                for tt in range(TT):
                    t = mm(ps[:, tt * P:(tt + 1) * P], [(V[:, tt, g * P:(g + 1) * P], wst[:, g, :])], t_v, t_ws)
                for tt in range(TT):
                    t2 = dve.do(op.tensor_tensor(
                        Y[:, 4 + g, tt * P:(tt + 1) * P], ps[:, tt * P:(tt + 1) * P], bs[:, g, :], ALU.add), t, t_bs)
                bank_free[bank].append(t2)
                y_ready[4 + g] = pool.do(op.tensor_tensor(Y[:, 4 + g, :], Y[:, 4 + g, :], U[:, g, :], ALU.mult), t2)
            return out_linear("ev_w_out", Y)
        pool_free = [None, None]

        def angle_tables(cosv, sinv, pos, freq, tmp, *after):
            big = 1.5 * 2.0 ** 23
            p1 = 6.28125
            p2 = float(np.float32(np.floor((2 * math.pi - p1) * 2 ** 20) / 2 ** 20))
            p3 = float(np.float32(2 * math.pi - p1 - p2))
            ang, k, r = tmp
            t = dve.do(op.tensor_scalar(ang, pos, freq, None, ALU.mult), *after)
            for dst, shift in ((sinv, 0.0), (cosv, 0.25)):
                for step in (
                        op.tensor_scalar(k, ang, 1.0 / (2 * math.pi), shift, ALU.mult, ALU.add),
                        op.tensor_scalar(k, k, big, None, ALU.add),
                        op.tensor_scalar(k, k, -big, None, ALU.add),
                        op.scalar_tensor_tensor(out=r, in0=k, scalar=-p1, in1=ang, op0=ALU.mult, op1=ALU.add),
                        op.scalar_tensor_tensor(out=r, in0=k, scalar=-p2, in1=r, op0=ALU.mult, op1=ALU.add),
                        op.scalar_tensor_tensor(out=r, in0=k, scalar=-p3, in1=r, op0=ALU.mult, op1=ALU.add),
                        op.tensor_scalar(r, r, 2 * math.pi * shift, -3.1415925, ALU.add, ALU.max),
                        op.tensor_scalar(r, r, 3.1415925, None, ALU.min)):
                    t = dve.do(step, t)
                    yield
                t = act.do(op.activation(dst, r, ACT.Sin), t)
            rotary_done.append(t)

        y_ready = {}
        rotary_done = []
        cosn, sinn, cosr, sinr = (wide[:, s, a:a + T2] for s in range(2) for a in (0, T2))

        def rotary_tables():
            lay = Layout(arena, hid_at + 2 * HALF_FC * T2 + 2 * T2, mixer_end)
            posf = lay(T2)
            tmp = [lay(T2) for _ in range(3)]
            t = small_load(posf.bitcast(I32), dram["positions"], dve.last, act.last, pe.last, pool.last)
            t = dve.do(op.tensor_copy(tmp[0], posf.bitcast(I32)), t)
            t = dve.do(op.tensor_copy(posf, tmp[0]), t)
            yield
            for _ in angle_tables(cosn, sinn, posf, k2("freq_n"), tmp, t):
                yield
            for _ in angle_tables(cosr, sinr, posf, k2("freq_r"), tmp, rotary_done[-1]):
                yield

        def odd_mixer(marks):
            L1 = Layout(arena, work1.at, work1.end)
            L2 = Layout(arena, work2.at, mixer_end)
            Y = L2(DC, T2)
            tmp3 = [L2(T2) for _ in range(3)]
            t_n = t_r = rotary_done[-1]
            base2 = L2.at
            Q = L1(4, T2)
            KC, VC = L1(T2), L1(T2)
            KS, KW = L1(2, T2), L1(2, T2)
            VS, VW = L1(TT, P), L1(TT, P)
            assert L1.at <= L1.end
            K2P, V2P = L2(2, T2), L2(2, T2)
            W2 = L2(2, P)
            GT = L2(TT, 24)
            KCT = L2(2, N_CMP + 1)
            VCT = L2(2, NSA_D)
            hcmp = L2(4, 32)
            bias = L2(8)
            PR = L2(2, 2, T2)
            PC = L2(2, 32)
            PT = L2(2, 2, T2)
            PCT = L2(2, P)
            rt = tmp3
            rt_free = [None] * 3
            rt_n = [0]

            def rope2(view, rot, cosv, sinv, t_in):
                i = rt_n[0] % 3
                rt_n[0] += 1
                bank, ps = all_banks.next()
                t = mm(ps, [(rot, view)], t_in)
                t2 = dve.do(op.tensor_tensor(rt[i], ps, sinv, ALU.mult), t, rt_free[i], t_n, t_r)
                bank_free[bank].append(t2)
                t = pool.do(op.tensor_tensor(view, view, cosv, ALU.mult), t, t_n, t_r)
                t = pool.do(op.tensor_tensor(view, view, rt[i], ALU.add), t, t2)
                rt_free[i] = t
                return t

            t_w2 = small_load(W2, dram["cmp_w2"].rearrange("a p n -> p a n"), *marks)
            for pair in range(2):
                w = Weights("od_w_in", 0, pair)
                for j in range(2):
                    c = 2 * pair + j
                    project(w, j * P, h_part, copy_to(Q[:, c, :]))
                    rope2(Q[:, c, :], k2("rot_n"), cosn, sinn, act.last)
                w.free(pe.last)
            w = Weights("od_w_in", 0, 2)
            project(w, 0, h_part, copy_to(KC))
            t_kc = rope2(KC, k2("rot_n"), cosn, sinn, act.last)
            project(w, P, h_part, copy_to(VC))
            t_vc = act.last
            w.free(pe.last)
            KX = PR[:, 0, 0, :]
            w = Weights("od_w_in", 0, 3)
            project(w, 0, h_part, copy_to(KX))
            t_ks = rope2(KX, k2("rot_n"), cosn, sinn, act.last)
            w.free(pe.last)
            w = Weights("od_w_in", 0, 4)
            token_major(w, P, lambda tt, ps, t: act.do(op.activation(VS[:, tt, :], ps, ACT.Copy), t))
            w.free(pe.last)
            KY = PR[:, 0, 1, :]
            w = Weights("od_w_in", 0, 5)
            project(w, 0, h_part, copy_to(KY))
            t_kw = rope2(KY, k2("rot_n"), cosn, sinn, act.last)
            w.free(pe.last)
            w = Weights("od_w_in", 0, 6)
            token_major(w, P, lambda tt, ps, t: act.do(op.activation(VW[:, tt, :], ps, ACT.Copy), t))
            w.free(pe.last)
            w = Weights("od_w_in", 0, 7)
            token_major(w, 3 * NSA_H, lambda tt, ps, t: act.do(op.activation(GT[:, tt, :], ps, ACT.Sigmoid), t))
            w.free(pe.last)
            t_gt = dve.do(op.tensor_scalar(GT[:, 0, 0:24:3], GT[:, 0, 0:24:3], k2("cmp_ok"), None, ALU.mult),
                          act.last)
            for g in range(2):
                for h in range(2):
                    lo, hi = slice(64 * g, 64 * g + 64), slice(64 * h, 64 * h + 64)
                    dve.do(op.tensor_copy(KS[hi, g, :], KX[lo, :]), t_ks)
                    dve.do(op.tensor_copy(KW[hi, g, :], KY[lo, :]), t_kw)
            for src, dst, t_s in ((KC, K2P, t_kc), (VC, V2P, t_vc)):
                for g in range(2):
                    lo = slice(64 * g, 64 * g + 64)
                    dve.do(op.tensor_copy(dst[0:64, g, :], src[lo, :]), t_s)
                    dve.do(op.tensor_copy(
                        dst[64:P, g, 0:T2 - 1], src[lo, 1:T2]), t_s)
            t_2p = dve.last
            for kv, (src, pos) in enumerate(((K2P, "k_pos"), (V2P, "v_pos"))):
                w = Weights("cmp_w1", kv, 0, False)
                bank, ps = all_banks.next()
                t = mm(ps[:, 0:1], [(w.v[:, j, :], vx(pos, j)) for j in range(16)], *w.ready)
                t_b = act.do(op.activation(bias[:, kv:kv + 1], ps[:, 0:1], ACT.Copy), t)
                bank_free[bank].append(t_b)
                for g in range(2):
                    bank, ps = all_banks.next()
                    t = mm(ps[:, 0:N_CMP],
                           [(w.v[:, j, :],
                             src[:, g, 2 * j:2 * j + CMP_STRIDE * (N_CMP - 1) + 1:CMP_STRIDE]) for j in range(16)], t_2p)
                    hc = hcmp[:, 2 * kv + g, 0:N_CMP]
                    t = act.do(op.activation(
                        hc, ps[:, 0:N_CMP], ACT.Gelu_apprx_tanh, bias=bias[:, kv:kv + 1]), t, t_b)
                    bank_free[bank].append(t)
                    bank, ps = all_banks.next()
                    if kv == 0:
                        t = mm(ps[:, 0:N_CMP], [(W2[:, 0, :], hc)], t, t_w2)
                        t = act.do(op.activation(KCT[:, g, 0:N_CMP], ps[:, 0:N_CMP], ACT.Copy), t)
                    else:
                        t = mm(ps[0:N_CMP, 0:NSA_D], [(hc, W2[:, 1, 0:NSA_D])], t, t_w2)
                        t = act.do(op.activation(VCT[0:N_CMP, g, :], ps[0:N_CMP, 0:NSA_D], ACT.Copy), t)
                    bank_free[bank].append(t)
                w.free(pe.last)
            gather()
            pr_free, pt_free, st_free = [None, None], [None, None], [None] * n_stat
            units = [dict(h=h, qt=qt) for h in range(NSA_H) for qt in range(TT)]
            scale = NSA_D ** -0.5
            tring = Ring([2, 6, 7])
            OBANK = 5

            def nsa_scores(i, u):
                h, qt = u["h"], u["qt"]
                g, hb = h // 4, slice(64 * (h % 2), 64 * (h % 2) + 64)
                q = Q[hb, h // 2, qt * P:(qt + 1) * P]
                n, x = (qt + 1) * P, i % 2
                st = stats[:, i % n_stat, :]
                bs, bw = 3 * x, 3 * x + 1
                ss, sw = take(bs), take(bw)
                bc, sc = tring.next()
                sc = sc[:, 0:N_CMP]
                tk = []
                for ps, kk in ((ss, KS), (sw, KW)):
                    if qt:
                        mm(ps[:, 0:qt * P], [(q, kk[hb, g, 0:qt * P])])
                    tk.append(mm(ps[:, qt * P:n], [(q, kk[hb, g, qt * P:n]), (ident, k2("causal"))]))
                a = K2["cmp_mask"][0] + qt * N_CMP
                tk.append(mm(sc, [(q, KCT[hb, g, 0:N_CMP]), (ident, con2[:, a:a + N_CMP])]))
                srcs = (sc, ss[:, 0:n], sw[:, 0:n])
                dsts = (PC[:, x, 0:N_CMP], PR[:, x, 0, 0:n], PR[:, x, 1, 0:n])
                order = (tk[2], tk[0], tk[1])
                for c in range(3):
                    t = dve.do(op.tensor_reduce(st[:, c:c + 1], srcs[c], AX.X, ALU.max), order[c],
                               st_free[i % n_stat])
                t = dve.do(op.tensor_scalar(st[:, 0:3], st[:, 0:3], -scale, None, ALU.mult), t)
                tx = []
                for c in range(3):
                    tx.append(act.do(op.activation(dsts[c], srcs[c], ACT.Exp, bias=st[:, c:c + 1],
                                                                 scale=scale, accum_out=st[:, 3 + c:4 + c]),
                                     t, pr_free[x], st_free[i % n_stat]))
                bank_free[bc].append(tx[0])
                bank_free[bs].append(tx[1])
                bank_free[bw].append(tx[2])
                t = dve.do(op.reciprocal(st[:, 3:6], st[:, 3:6]), tx[2])
                t = dve.do(op.tensor_tensor(st[:, 3:6], st[:, 3:6], GT[:, qt, 3 * h:3 * h + 3], ALU.mult), t, t_gt)
                out_t = [dve.do(op.tensor_scalar(dsts[c], dsts[c], st[:, 3 + c:4 + c], None, ALU.mult), t)
                         for c in (0, 1)]
                out_t.append(act.do(op.activation(dsts[2], dsts[2], ACT.Copy, scale=st[:, 5:6]), t))
                st_free[i % n_stat] = out_t[-1]
                u["ready"] = out_t
                u["dsts"] = dsts

            def nsa_turn(i, u):
                x, nt = i % 2, u["qt"] + 1
                pe.wait(*u["ready"])
                copied = []
                for c in range(2):
                    bank, ps = tring.next()
                    for k in range(nt):
                        t = pe.do(op.transpose(ps[:, k * P:(k + 1) * P],
                                                                         PR[:, x, c, k * P:(k + 1) * P], ident))
                    if c == 0:
                        t = dve.do(op.tensor_copy(PT[:, x, 0, 0:nt * P], ps[:, 0:nt * P]), t, pt_free[x])
                    else:
                        t = act.do(op.activation(PT[:, x, 1, 0:nt * P], ps[:, 0:nt * P], ACT.Copy), t,
                                   pt_free[x])
                    bank_free[bank].append(t)
                    copied.append(t)
                bank, ct = tring.next()
                ct = ct[0:N_CMP, 0:P]
                t = pe.do(op.transpose(ct, PC[:, x, 0:N_CMP], ident))
                pr_free[x] = t
                t = dve.do(op.tensor_copy(PCT[0:N_CMP, x, :], ct), t, pt_free[x])
                bank_free[bank].append(t)
                copied.append(t)
                u["copied"] = copied

            def nsa_values(i, u):
                h, qt = u["h"], u["qt"]
                g, hb = h // 4, slice(64 * (h % 2), 64 * (h % 2) + 64)
                x, nt = i % 2, qt + 1
                if h % 2 == 0 and qt == 0:
                    take(OBANK)
                o = psum[hb, OBANK * BANK + qt * P:OBANK * BANK + (qt + 1) * P]
                vcols = slice(64 * g, 64 * g + 64)
                pairs = [(VS[:, k, vcols], PT[:, x, 0, k * P:(k + 1) * P]) for k in range(nt)]
                pairs += [(VW[:, k, vcols], PT[:, x, 1, k * P:(k + 1) * P]) for k in range(nt)]
                pairs += [(VCT[0:N_CMP, g, :], PCT[0:N_CMP, x, :])]
                t = mm(o, pairs, *u["copied"])
                pt_free[x] = t
                if h % 2 == 1 and qt == TT - 1:
                    t = y_ready[h // 2] = act.do(op.activation(Y[:, h // 2, :], psum[:, OBANK * BANK:(OBANK + 1) * BANK], ACT.Copy), t)
                    bank_free[OBANK].append(t)

            for i, u in enumerate(units):
                nsa_scores(i, u)
                if i > 1:
                    nsa_values(i - 2, units[i - 2])
                if i:
                    nsa_turn(i - 1, units[i - 1])
            n = len(units)
            nsa_values(n - 2, units[-2])
            nsa_turn(n - 1, units[-1])
            nsa_values(n - 1, units[-1])
            marks = [q.last for q in (pe, act, dve, pool)]
            for q in (act, dve, pool):
                q.wait(*marks)
            L1 = Layout(arena, work1.at, work1.end)
            L2 = Layout(arena, base2, mixer_end)
            RQ, RK, RV = L1(4, T2), L1(4, T2), L1(TT, T2)
            DEC = L2(RET_H, T2)
            eps5 = L2(1)
            ST = L2(2, TT, T2)
            GS = [cosn, sinn]
            RO = tmp3[0:2]
            t_dec = small_load(DEC, dram["decay"], *marks)
            for blk, dst in ((8, RQ), (10, RK)):
                for c in range(4):
                    if c % 2 == 0:
                        w = Weights("od_w_in", 0, blk + c // 2)
                    project(w, (c % 2) * P, h_part, copy_to(dst[:, c, :]))
                    rope2(dst[:, c, :], k2("rot_r"), cosr, sinr, act.last)
                    if c % 2 == 1:
                        w.free(pe.last)
            for pair in range(2):
                w = Weights("od_w_in", 0, 12 + pair)
                token_major(w, 256, lambda tt, ps, t, a=256 * pair: act.do(
                    op.activation(RV[:, tt, a:a + 256], ps, ACT.Copy), t))
                w.free(pe.last)
            gather()
            st_f, ro_f = [None, None], [None, None]
            t_eps = pool.do(op.memset(eps5, 1e-5))
            for h in range(RET_H):
                x = h % 2
                ready = []
                for j in range(TT):
                    bank, ps = all_banks.next()
                    n = T2 - j * P
                    t = mm(ps[:, 0:n], [(RK[:, h, j * P:(j + 1) * P], RQ[:, h, j * P:T2])])
                    t = dve.do(op.tensor_tensor(
                        ST[:, x, j, 0:n], ps[:, 0:n], DEC[:, h, 0:n], ALU.mult), t, t_dec, st_f[x])
                    bank_free[bank].append(t)
                    ready.append(t)
                bank, ps = all_banks.next()
                for i in range(TT):
                    t = mm(ps[:, i * P:(i + 1) * P],
                           [(RV[:, j, h * P:(h + 1) * P], ST[:, x, j, (i - j) * P:(i - j + 1) * P]) for j in range(i + 1)],
                           *ready)
                st_f[x] = t
                o = RO[x]
                t = act.do(op.activation(o, ps, ACT.Copy), t, ro_f[x])
                bank_free[bank].append(t)
                bank, ps = all_banks.next()
                t = mm(ps, [(ones, o)], t)
                t = dve.do(op.scalar_tensor_tensor(out=o, in0=ps, scalar=-1.0 / P, in1=o,
                                                                       op0=ALU.mult, op1=ALU.add), t)
                bank_free[bank].append(t)
                sq, r = row[:, x, :], rstd[:, x, :]
                t_sq = act.do(op.activation(sq, o, ACT.Square), t, ro_f[x])
                bank, ps = all_banks.next()
                t2 = mm(ps, [(ones, sq)], t_sq)
                t2 = rsqrt(r, ps, P, t2, t_eps, eps=eps5)
                bank_free[bank].append(t2)
                gs = GS[x]
                if h % 2 == 0:
                    w = Weights("od_w_in", 0, 14 + h // 2)
                project(w, (h % 2) * P, h_part, lambda ps, t, gs=gs, x=x: act.do(
                    op.activation(gs, ps, ACT.Silu), t, ro_f[x]))
                t_gs = act.last
                if h % 2 == 1:
                    w.free(pe.last)
                t2 = dve.do(op.scalar_tensor_tensor(
                    out=r, in0=o, scalar=vx("gn_g", h), in1=r, op0=ALU.mult, op1=ALU.mult), t2)
                t2 = pool.do(op.tensor_tensor(Y[:, 4 + h, :], r, gs, ALU.mult), t2, t_gs)
                ro_f[x] = y_ready[4 + h] = t2
            return out_linear("od_w_out", Y)

        def swiglu(layer, between):
            L1 = Layout(arena, work1.at, work1.end)
            L2 = Layout(arena, work2.at, mixer_end)
            gs = Layout(arena, hid_at + 2 * HALF_FC * T2, mixer_end)(2, T2)
            g_free = [[], []]
            for half in range(2):
                for m in range(HALF_FC):
                    w = Weights("ffn_up", layer, half * HALF_FC + m)
                    x = m % 2
                    g = gs[:, x, :]
                    project(w, 0, h_part, lambda ps, t: act.do(op.activation(g, ps, ACT.Silu), t, *g_free[x]))
                    t_g = act.last
                    project(w, P, h_part, lambda ps, t: dve.do(op.tensor_tensor(g, g, ps, ALU.mult), t, t_g))
                    w.free(pe.last)
                    g_free[x] = split(*hid2_part(m, 0, T2), g, dve.last)
                    hid_ready[m, 0] = g_free[x][1]
                    for _ in range(2):
                        next(between, None)
                sq = Squares(DC, D, on_pool=True)
                for m in range(DC):
                    w = Weights("ffn_down", 2 * layer + half, m)
                    if half == 0:
                        project(w, 0, hid2_part, copy_to(MX[:, m, :]), nk=HALF_FC)
                    else:
                        project(w, 0, hid2_part, lambda ps, t: dve.do(op.tensor_tensor(
                            MX[:, m, :], MX[:, m, :], ps, ALU.add), t), nk=HALF_FC)
                        sq.flush()
                        sq.add(MX[:, m, :], dve.last)
                    w.free(pe.last)
            for _ in between:
                pass
            return sq

        if stop is None or stop[0] == "b2":
            for layer in range(DEPTH):
                h_ready.clear()
                hid_ready.clear()
                marks = [q.last for q in (pe, act, dve, pool)]
                h_ready |= pre_norm(squares, "mix_pre")
                sq = even_mixer(marks) if layer == 0 else odd_mixer(marks)
                squares = post_norm(sq, "mix_post")
                if stop == ("b2", layer, "mix"):
                    squares.flush()
                    break
                h_ready |= pre_norm(squares, "ffn_pre")
                sq = swiglu(layer, rotary_tables() if layer == 0 else iter(()))
                squares = post_norm(sq, "ffn_post")
                if stop == ("b2", layer):
                    break

        sp.wait(*[q.last for q in (dve, pool, act)])
        sp.dma(out.rearrange("(c p) t -> p c t", p=P), X, out_sem)
        sp.wait((out_sem, 16))

        if plan is None:
            return used
        assert len(used) == len(plan)
        block = ctx.enter_context(nc.Block())

        @block.sync
        def _(e):
            sp.run(e)

        @block.tensor
        def _(e):
            pe.run(e)

        @block.scalar
        def _(e):
            act.run(e)

        @block.vector
        def _(e):
            dve.run(e)

        @block.gpsimd
        def _(e):
            pool.run(e)


def const_arrays():
    f32 = np.float32

    def axial(dr):
        q = dr // 4
        freqs = (f32(10000.0) ** (-np.arange(q, dtype=f32) / f32(q))).astype(f32)
        rows = np.repeat(np.arange(N_LAT // GRID_W), GRID_W).astype(f32)
        cols = np.tile(np.arange(GRID_W), N_LAT // GRID_W).astype(f32)
        ar, ac = np.outer(freqs, rows).astype(f32), np.outer(freqs, cols).astype(f32)
        ang = np.concatenate([ar, ar, ac, ac])
        rot = np.zeros((dr, dr), f32)
        for base in (0, 2 * q):
            for i in range(q):
                rot[base + q + i, base + i] = -1.0
                rot[base + i, base + q + i] = 1.0
        return np.cos(ang).astype(f32), np.sin(ang).astype(f32), rot

    one = np.zeros((P, NK1), f32)

    def put(arr, cols, name, rows, v):
        a, _ = cols[name]
        arr[rows, a:a + v.shape[1]] = v

    cb, sb_, rb = axial(DH_B)
    ca, sa, ra = axial(ROPE_A)
    for s in range(2):
        rows = slice(64 * s, 64 * s + 64)
        put(one, K1, "cos_b", rows, cb)
        put(one, K1, "sin_b", rows, sb_)
        a = K1["rot_b"][0] + 64 * s
        one[rows, a:a + 64] = rb
    rows = slice(NOPE_A, NOPE_A + ROPE_A)
    put(one, K1, "cos_a", rows, ca)
    put(one, K1, "sin_a", rows, sa)
    put(one, K1, "rot_a", rows, ra)

    two = np.zeros((P, NK2), f32)
    i = np.arange(P)
    put(two, K2, "causal", slice(0, P), np.where(i[None, :] <= i[:, None], 0.0, MASKED).astype(f32))
    for t in range(TT):
        ok = (np.arange(N_CMP) * CMP_STRIDE + CMP_BLOCK - 1)[None, :] <= (t * P + i)[:, None]
        a = K2["cmp_mask"][0] + t * N_CMP
        two[:, a:a + N_CMP] = np.where(ok, 0.0, MASKED)
    half = NSA_ROPE // 2
    rn = np.zeros((P, P), f32)
    for b in (0, 64):
        for k in range(half):
            rn[b + half + k, b + k] = -1.0
            rn[b + k, b + half + k] = 1.0
    put(two, K2, "rot_n", slice(0, P), rn)
    rr = np.zeros((P, P), f32)
    for k in range(64):
        rr[64 + k, k] = -1.0
        rr[k, 64 + k] = 1.0
    put(two, K2, "rot_r", slice(0, P), rr)

    def inv(theta, dim):
        e = (np.arange(0, dim, 2, dtype=f32) / f32(dim)).astype(f32)
        return (f32(1.0) / (f32(theta) ** e)).astype(f32)

    fn = np.zeros((P, 1), f32)
    for b in (0, 64):
        for k in range(NSA_ROPE):
            fn[b + k, 0] = inv(NSA_THETA, NSA_ROPE)[k % half]
    put(two, K2, "freq_n", slice(0, P), fn)
    put(two, K2, "freq_r", slice(0, P), np.tile(inv(RET_THETA, RET_D), 2)[:, None])
    put(two, K2, "cmp_ok", slice(0, P), (i >= CMP_BLOCK - 1).astype(f32)[:, None])
    a = K2["pool_count"][0]
    for g, win in enumerate(POOL_WINDOWS):
        two[:, a + 16 * g:a + 16 * g + 16] = win / np.minimum(np.arange(16) + 1, win)
    h = np.arange(RET_H)
    lg = np.log1p(-np.exp2(-5.0 - h))
    rel = np.arange(T2)[None, :] - i[:, None]
    dec = np.where(rel[None] >= 0, np.exp(np.maximum(rel, 0)[None] * lg[:, None, None]), 0.0) * RET_D ** -0.5
    decay = np.ascontiguousarray(dec.transpose(1, 0, 2)).astype(f32)
    return one, two, decay.reshape(P, RET_H * T2), np.eye(P, dtype=f32)


def pack(name, layers):
    nk, parts = ROWS[name] // P, []
    for w in layers:
        for ranges in blocks_of(name):
            for_block = np.concatenate([w[:, a:b] for a, b in ranges], axis=1)
            parts.append(for_block.reshape(nk, P, -1).transpose(1, 0, 2).reshape(-1))
    return np.concatenate(parts)


def cols_of(v):
    return np.ascontiguousarray(v.reshape(-1, P).T)


def spread(v):
    return np.ascontiguousarray(np.broadcast_to(v[None], (P, *v.shape)))


def lay_out(i):
    f = {k: np.asarray(v) for k, v in i.items()}
    out = {}
    two = range(DEPTH)
    cat = np.concatenate
    out["x_t"] = np.ascontiguousarray(cat([f["ctx"][0], f["x"][0]], axis=0).T)
    out["c_pair"] = np.ascontiguousarray(np.stack([f["c"][0], f["c_ctx"]], axis=1))
    out["w_ada"] = np.concatenate([
        (b.reshape(DC, P, 256).transpose(1, 0, 2) if l == 0 and i in ADA_ON_PE else b.T.reshape(2, P, D).transpose(1, 0, 2)
         ).reshape(-1) for l in two for i, b in enumerate(np.split(f["w_ada"][l], 24, axis=1))])
    out["c_wide"] = spread(np.stack([f["c"][0], f["c_ctx"]]))
    out["w_in"] = pack("w_in", f["w_in"])
    out["w_uq"] = pack("w_uq", f["w_uq"])
    out["w_ukv"] = pack("w_ukv", f["w_ukv"])
    out["w_br"] = pack("w_br", [cat([f["w_br_a"][l], f["w_br_b"][l]], axis=1) for l in two])
    out["w_out"] = pack("w_out", f["w_out"])
    out["w_up"] = pack("w_up", f["w_up"])
    out["w_down"] = pack("w_down", [h for l in two for h in np.split(f["w_down"][l], 2)])
    out["ffn_up"] = pack("ffn_up", [cat([f["ffn_w_gate_2"][l], f["ffn_w_up_2"][l]], axis=1) for l in two])
    out["ffn_down"] = pack("ffn_down", [h for l in two for h in np.split(f["ffn_w_down_2"][l], 2)])
    for n in ("ev_w_in", "ev_w_out", "od_w_in", "od_w_out"):
        out[n] = pack(n, f[n + "_2"])
    out["vec1"] = np.stack([cat([cols_of(f[n][l].reshape(-1)) for n, _ in VEC1], axis=1) for l in two])
    out["lam"] = np.stack([np.stack([spread(np.stack([f["lam_" + a + "1"][l], f["lam_" + a + "2"][l]]))
                                     for a in "qk"]) for l in two])
    names = {"mix_pre": "ln_mix_pre_2", "mix_post": "ln_mix_post_2", "ffn_pre": "ln_ffn_pre_2", "ffn_post": "ln_ffn_post_2"}
    out["vec2"] = np.stack([cat([cols_of(f[names[n]][l]) for n, _ in VEC2], axis=1) for l in two])
    vx = {"pool_scale": f["ev_pool_scale_2"][0], "gn_g": f["od_ret_gn_g_2"][0], "g_final": f["g_final"],
          "k_pos": f["od_cmp_k_pos_2"][0].reshape(-1), "v_pos": f["od_cmp_v_pos_2"][0].reshape(-1)}
    out["vec2x"] = cat([cols_of(vx[n]) for n, _ in VEC2X], axis=1)
    out["const1"], out["const2"], out["decay"], out["ident"] = const_arrays()
    out["sgu_gb"] = spread(np.stack([f["ev_sgu_ln_g_2"][0], f["ev_sgu_ln_b_2"][0]]))
    out["sgu_bs"] = spread(f["ev_sgu_b_2"][0])
    out["sgu_wt"] = np.ascontiguousarray(f["ev_sgu_w_2"][0].transpose(0, 2, 1))
    out["pool_w"] = np.ascontiguousarray(f["ev_pool_w_2"][0])
    out["positions"] = spread(f["positions_2"][0])
    w1 = [f["od_cmp_k_w1_2"][0], f["od_cmp_v_w1_2"][0]]
    out["cmp_w1"] = pack("cmp_w1", w1)
    w2 = [f["od_cmp_k_w2_2"][0], f["od_cmp_v_w2_2"][0]]
    out["cmp_w2"] = np.stack([cat([w, w], axis=1) for w in w2])
    return {k: np.ascontiguousarray(v) for k, v in out.items()}


def kernel(**inputs):
    import concourse.bacc as bacc
    from concourse.bass_utils import run_bass_kernel_spmd

    arrays = lay_out(inputs)
    plan = None
    for _ in range(2):
        nc = bacc.Bacc("TRN2", target_bir_lowering=False, num_devices=1,
                       dynamic_dma_scratch_size=64)
        dram = {n: nc.dram_tensor(n + "_dram", a.shape, mybir.dt.from_np(a.dtype), kind="ExternalInput").ap()
                for n, a in arrays.items()}
        out = nc.dram_tensor("out_dram", (D, T2), F32, kind="ExternalOutput").ap()
        plan = build(nc, dram, out, plan, STOP)
    r = run_bass_kernel_spmd(nc, [{n + "_dram": a for n, a in arrays.items()}], core_ids=[0])
    return np.ascontiguousarray(r.results[0]["out_dram"].T)[None]


STOP = None
```
